# Optimizing a Trainium2 kernel written in Bass

```python
import math
import jax, jax.numpy as jnp
from jax import lax
import numpy as np

D_MODEL = 1024
BATCH = 1
SEQ = 512
DEPTH = 1
DEC_BATCH = 8
DEC_SEQ = 4
PAST_LEN = 4096
PAGE_SIZE = 128

S5_WIDTH = D_MODEL // 2
S5_GROUP = 16
S5_GROUPS = S5_WIDTH // S5_GROUP
S5_STATE = 64
CONV_WIDTH = D_MODEL // 2
CONV_K = 31
N_MEM = 256
XA_HEADS = 4
XA_HEAD_DIM = D_MODEL // 8
XA_WIDTH = XA_HEADS * XA_HEAD_DIM
N_BRANCH = 3
IN_WIDTH = S5_WIDTH + 2 * CONV_WIDTH + XA_WIDTH + N_BRANCH * D_MODEL
PEER_HEADS = 8
PEER_NKEYS = 128
PEER_N_EXPERTS = PEER_NKEYS * PEER_NKEYS
PEER_KEY_DIM = D_MODEL // 4
PEER_HALF = PEER_KEY_DIM // 2
PEER_TOPK = 16
PEER_BLOCK = 256
RMS_EPS = 1e-6
LN_EPS = 1e-5

kernel_name = 'hybrid_s5_conformer_memxattn_peer_step'

def _rmsnorm(x, g):
    xf = x.astype(jnp.float32)
    y = xf * lax.rsqrt(jnp.mean(xf * xf, axis=-1, keepdims=True) + RMS_EPS)
    return (y * g.astype(jnp.float32)).astype(x.dtype)

def _layernorm(x, g, b):
    xf = x.astype(jnp.float32)
    xc = xf - jnp.mean(xf, axis=-1, keepdims=True)
    var = jnp.mean(xc * xc, axis=-1, keepdims=True)
    y = xc * lax.rsqrt(var + LN_EPS) * g.astype(jnp.float32) + b.astype(jnp.float32)
    return y.astype(x.dtype)

def _s5_discretize(log_dt, a_re, a_im, b_re, b_im):
    f32 = jnp.float32
    lam = lax.complex(a_re.astype(f32), a_im.astype(f32))
    dt = jnp.exp(log_dt.astype(f32))[:, None]
    lam_bar = jnp.exp(lam * dt)
    b_mat = lax.complex(b_re.astype(f32), b_im.astype(f32))
    b_bar = ((lam_bar - 1.0) / lam)[:, :, None] * b_mat
    return lam_bar, b_bar

def _s5_scan(u, h0, lam_bar, b_bar, c_re, c_im, d):
    bsz, t = u.shape[0], u.shape[1]
    ug = u.astype(jnp.float32).reshape(bsz, t, S5_GROUPS, S5_GROUP)
    bu = jnp.einsum('gnc,btgc->btgn', b_bar, ug.astype(jnp.complex64))
    bu = bu.at[:, 0].add(lam_bar[None] * h0)
    a = jnp.broadcast_to(lam_bar, bu.shape)

    def combine(e1, e2):
        a1, b1 = e1
        a2, b2 = e2
        return a2 * a1, a2 * b1 + b2

    _, states = lax.associative_scan(combine, (a, bu), axis=1)
    c_mat = lax.complex(c_re.astype(jnp.float32), c_im.astype(jnp.float32))
    y = jnp.einsum('gcn,btgn->btgc', c_mat, states).real + d.astype(jnp.float32) * ug
    return y.reshape(bsz, t, S5_WIDTH).astype(u.dtype), states[:, -1]

def _conv_module(a, conv_state, dw_w, dw_b, ln_g, ln_b):
    xin = jnp.concatenate([conv_state.astype(a.dtype), a], axis=1)
    y = lax.conv_general_dilated(
        xin, dw_w.astype(a.dtype)[:, None, :], window_strides=(1,), padding='VALID',
        dimension_numbers=('NWC', 'WIO', 'NWC'), feature_group_count=CONV_WIDTH)
    y = _layernorm(y + dw_b.astype(a.dtype), ln_g, ln_b)
    return jax.nn.silu(y), xin[:, -(CONV_K - 1):]

def _mem_kv(mem, mem_norm_g, w_mem_k, w_mem_v):
    bsz = mem.shape[0]
    m = _rmsnorm(mem, mem_norm_g)
    k = (m @ w_mem_k).reshape(bsz, N_MEM, XA_HEADS, XA_HEAD_DIM)
    v = (m @ w_mem_v).reshape(bsz, N_MEM, XA_HEADS, XA_HEAD_DIM)
    return k, v

def _cross_attend(q, k, v):
    s = jnp.einsum('bthd,bmhd->bhtm', q, k).astype(jnp.float32) * (XA_HEAD_DIM ** -0.5)
    p = jax.nn.softmax(s, axis=-1).astype(v.dtype)
    return jnp.einsum('bhtm,bmhd->bthd', p, v)

def _peer_block(xb, w_q, sub_keys, u_tab, v_tab):
    tb = xb.shape[0]
    q = (xb @ w_q).reshape(tb, PEER_HEADS, 2, PEER_HALF).astype(jnp.float32)
    s = jnp.einsum('thpc,pkc->thpk', q, sub_keys.astype(jnp.float32))
    sv, si = lax.top_k(s, PEER_TOPK)
    cand = sv[:, :, 0, :, None] + sv[:, :, 1, None, :]
    cv, ci = lax.top_k(cand.reshape(tb, PEER_HEADS, PEER_TOPK * PEER_TOPK), PEER_TOPK)
    i1 = jnp.take_along_axis(si[:, :, 0], ci // PEER_TOPK, axis=-1)
    i2 = jnp.take_along_axis(si[:, :, 1], ci % PEER_TOPK, axis=-1)
    experts = i1 * PEER_NKEYS + i2
    gate = jax.nn.softmax(cv, axis=-1)
    u = u_tab[experts]
    act = jax.nn.gelu(jnp.einsum('thkd,td->thk', u, xb).astype(jnp.float32), approximate=False)
    w = (gate * act).astype(xb.dtype)
    return jnp.einsum('thk,thkd->td', w, v_tab[experts])

def _peer(x, w_q, sub_keys, u_tab, v_tab):
    bsz, t, d = x.shape
    n = bsz * t
    nblk = -(-n // PEER_BLOCK)
    flat = jnp.pad(x.reshape(n, d), ((0, nblk * PEER_BLOCK - n), (0, 0)))
    out = lax.map(lambda xb: _peer_block(xb, w_q, sub_keys, u_tab, v_tab),
                  flat.reshape(nblk, PEER_BLOCK, d))
    return out.reshape(nblk * PEER_BLOCK, d)[:n].reshape(bsz, t, d)

def _trunk_layer(h, mem_k, mem_v, ssm_h0, conv_state,
                 norm1_g, w_in, b_in, s5_log_dt, s5_a_re, s5_a_im, s5_b_re, s5_b_im,
                 s5_c_re, s5_c_im, s5_d, s5_glu_w, s5_glu_b, w_s5_proj,
                 conv_dw_w, conv_dw_b, conv_ln_g, conv_ln_b, w_conv_proj,
                 w_xa_proj, w_out, norm2_g, peer_w_q, peer_sub_keys, peer_u, peer_v):
    bsz, t, d = h.shape
    n = _rmsnorm(h, norm1_g)
    z = n @ w_in + b_in
    o1 = S5_WIDTH
    o2 = o1 + 2 * CONV_WIDTH
    o3 = o2 + XA_WIDTH
    u_s5, a_pre, q, gl = z[..., :o1], z[..., o1:o2], z[..., o2:o3], z[..., o3:]

    lam_bar, b_bar = _s5_discretize(s5_log_dt, s5_a_re, s5_a_im, s5_b_re, s5_b_im)
    y_s5, ssm_new = _s5_scan(u_s5, ssm_h0, lam_bar, b_bar, s5_c_re, s5_c_im, s5_d)
    zz = jax.nn.gelu(y_s5, approximate=False)
    br_s5 = (zz * jax.nn.sigmoid(zz @ s5_glu_w + s5_glu_b)) @ w_s5_proj

    a = a_pre[..., :CONV_WIDTH] * jax.nn.sigmoid(a_pre[..., CONV_WIDTH:])
    c_out, conv_new = _conv_module(a, conv_state, conv_dw_w, conv_dw_b, conv_ln_g, conv_ln_b)
    br_conv = c_out @ w_conv_proj

    o = _cross_attend(q.reshape(bsz, t, XA_HEADS, XA_HEAD_DIM), mem_k, mem_v)
    br_xa = o.reshape(bsz, t, XA_WIDTH) @ w_xa_proj

    g = jax.nn.sigmoid(gl.astype(jnp.float32)).astype(h.dtype).reshape(bsz, t, N_BRANCH, d)
    merged = g[:, :, 0] * br_s5 + g[:, :, 1] * br_conv + g[:, :, 2] * br_xa
    h = h + merged @ w_out

    h = h + _peer(_rmsnorm(h, norm2_g), peer_w_q, peer_sub_keys, peer_u, peer_v)
    return h, ssm_new, conv_new

def setup_inputs(seed: int = 0) -> dict:
    key = jax.random.key(seed)
    ks = list(jax.random.split(key, 48))

    def nrm(shape, scale):
        return scale * jax.random.normal(ks.pop(), shape, jnp.float32)

    L = DEPTH
    G, N = S5_GROUPS, S5_STATE
    n_idx = jnp.arange(N, dtype=jnp.float32)
    return {
        'x_prompt': nrm((BATCH, SEQ, D_MODEL), 1.0),
        'x_sample': nrm((DEC_BATCH, DEC_SEQ, D_MODEL), 1.0),
        'mem_prompt': nrm((BATCH, N_MEM, D_MODEL), 1.0),
        'state_ssm_re': nrm((L, DEC_BATCH, G, N), 0.5),
        'state_ssm_im': nrm((L, DEC_BATCH, G, N), 0.5),
        'state_conv': nrm((L, DEC_BATCH, CONV_K - 1, CONV_WIDTH), 0.5),
        'cache_mem_k': nrm((L, DEC_BATCH, N_MEM, XA_HEADS, XA_HEAD_DIM), 1.0),
        'cache_mem_v': nrm((L, DEC_BATCH, N_MEM, XA_HEADS, XA_HEAD_DIM), 1.0),
        'norm1_g': 1.0 + nrm((L, D_MODEL), 0.02),
        'w_in': nrm((L, D_MODEL, IN_WIDTH), D_MODEL ** -0.5),
        'b_in': nrm((L, IN_WIDTH), 0.02),
        's5_log_dt': jax.random.uniform(ks.pop(), (L, G), jnp.float32,
                                        minval=math.log(1e-3), maxval=math.log(1e-1)),
        's5_a_re': -0.5 * jnp.exp(nrm((L, G, N), 0.05)),
        's5_a_im': math.pi * n_idx + nrm((L, G, N), 0.01),
        's5_b_re': nrm((L, G, N, S5_GROUP), S5_GROUP ** -0.5),
        's5_b_im': nrm((L, G, N, S5_GROUP), S5_GROUP ** -0.5),
        's5_c_re': nrm((L, G, S5_GROUP, N), N ** -0.5),
        's5_c_im': nrm((L, G, S5_GROUP, N), N ** -0.5),
        's5_d': nrm((L, G, S5_GROUP), 1.0),
        's5_glu_w': nrm((L, S5_WIDTH, S5_WIDTH), S5_WIDTH ** -0.5),
        's5_glu_b': nrm((L, S5_WIDTH), 0.02),
        'w_s5_proj': nrm((L, S5_WIDTH, D_MODEL), S5_WIDTH ** -0.5),
        'conv_dw_w': nrm((L, CONV_K, CONV_WIDTH), CONV_K ** -0.5),
        'conv_dw_b': nrm((L, CONV_WIDTH), 0.02),
        'conv_ln_g': 1.0 + nrm((L, CONV_WIDTH), 0.02),
        'conv_ln_b': nrm((L, CONV_WIDTH), 0.02),
        'w_conv_proj': nrm((L, CONV_WIDTH, D_MODEL), CONV_WIDTH ** -0.5),
        'mem_norm_g': 1.0 + nrm((L, D_MODEL), 0.02),
        'w_mem_k': nrm((L, D_MODEL, XA_WIDTH), D_MODEL ** -0.5),
        'w_mem_v': nrm((L, D_MODEL, XA_WIDTH), D_MODEL ** -0.5),
        'w_xa_proj': nrm((L, XA_WIDTH, D_MODEL), XA_WIDTH ** -0.5),
        'w_out': nrm((L, D_MODEL, D_MODEL), D_MODEL ** -0.5),
        'norm2_g': 1.0 + nrm((L, D_MODEL), 0.02),
        'peer_w_q': nrm((L, D_MODEL, PEER_HEADS * PEER_KEY_DIM), D_MODEL ** -0.5),
        'peer_sub_keys': nrm((L, 2, PEER_NKEYS, PEER_HALF), PEER_HALF ** -0.5),
        'peer_u': nrm((L, PEER_N_EXPERTS, D_MODEL), D_MODEL ** -0.5),
        'peer_v': nrm((L, PEER_N_EXPERTS, D_MODEL), 0.3),
        'final_norm_g': 1.0 + nrm((D_MODEL,), 0.02),
    }

def reference(x_prompt, x_sample, mem_prompt, state_ssm_re, state_ssm_im, state_conv,
              cache_mem_k, cache_mem_v, norm1_g, w_in, b_in, s5_log_dt, s5_a_re, s5_a_im,
              s5_b_re, s5_b_im, s5_c_re, s5_c_im, s5_d, s5_glu_w, s5_glu_b, w_s5_proj,
              conv_dw_w, conv_dw_b, conv_ln_g, conv_ln_b, w_conv_proj, mem_norm_g,
              w_mem_k, w_mem_v, w_xa_proj, w_out, norm2_g, peer_w_q, peer_sub_keys,
              peer_u, peer_v, final_norm_g):
    hp, hs = x_prompt, x_sample
    bp = x_prompt.shape[0]
    re_p, im_p, conv_p, mk_p, mv_p, re_s, im_s, conv_s = [], [], [], [], [], [], [], []
    for l in range(DEPTH):
        lw = (norm1_g[l], w_in[l], b_in[l], s5_log_dt[l], s5_a_re[l], s5_a_im[l],
              s5_b_re[l], s5_b_im[l], s5_c_re[l], s5_c_im[l], s5_d[l], s5_glu_w[l],
              s5_glu_b[l], w_s5_proj[l], conv_dw_w[l], conv_dw_b[l], conv_ln_g[l],
              conv_ln_b[l], w_conv_proj[l], w_xa_proj[l], w_out[l], norm2_g[l],
              peer_w_q[l], peer_sub_keys[l], peer_u[l], peer_v[l])
        mk, mv = _mem_kv(mem_prompt, mem_norm_g[l], w_mem_k[l], w_mem_v[l])
        h0p = jnp.zeros((bp, S5_GROUPS, S5_STATE), jnp.complex64)
        cs0p = jnp.zeros((bp, CONV_K - 1, CONV_WIDTH), hp.dtype)
        hp, ssm_p, cnv_p = _trunk_layer(hp, mk, mv, h0p, cs0p, *lw)
        re_p.append(ssm_p.real)
        im_p.append(ssm_p.imag)
        conv_p.append(cnv_p)
        mk_p.append(mk)
        mv_p.append(mv)
        h0s = lax.complex(state_ssm_re[l].astype(jnp.float32), state_ssm_im[l].astype(jnp.float32))
        hs, ssm_s, cnv_s = _trunk_layer(hs, cache_mem_k[l], cache_mem_v[l], h0s, state_conv[l], *lw)
        re_s.append(ssm_s.real)
        im_s.append(ssm_s.imag)
        conv_s.append(cnv_s)
    y_prompt = _rmsnorm(hp, final_norm_g)
    y_sample = _rmsnorm(hs, final_norm_g)
    return (y_prompt, y_sample, jnp.stack(re_p), jnp.stack(im_p), jnp.stack(conv_p),
            jnp.stack(mk_p), jnp.stack(mv_p), jnp.stack(re_s), jnp.stack(im_s), jnp.stack(conv_s))


_drawn_inputs = setup_inputs


def setup_inputs(seed=0):
    import zlib

    import numpy as np

    out = dict(_drawn_inputs(seed))
    spreads = {}
    factors = {'s5_glu_b': 31.717,
     'conv_dw_b': 2.809,
     'conv_ln_g': 3.864,
     'conv_ln_b': 3.967,
     'mem_norm_g': 2.942,
     'norm2_g': 2.705,
     'final_norm_g': 8.542}
    for name, (base, spread) in spreads.items():
        noise = np.random.default_rng([zlib.crc32(name.encode()), seed]).standard_normal(out[name].shape)
        drawn = base * np.exp(spread * noise) if base else spread * noise
        out[name] = __import__('jax').numpy.asarray(drawn.astype(out[name].dtype))
    for name, factor in factors.items():
        out[name] = (out[name] * factor).astype(out[name].dtype)
    return out
```

```python
from contextlib import ExitStack

import concourse.bass as bass
from concourse import mybir

F32 = mybir.dt.float32
I32 = mybir.dt.int32
U32 = mybir.dt.uint32
ALU = mybir.AluOpType
ACT = mybir.ActivationFunctionType
AX = mybir.AxisListType

P = 128
D = 1024
KD = D // P
HALF = 512 // P
SEQ, NB, NT = 512, 8, 4
TOK = SEQ + NB * NT
HT = TOK // 2
G, N, CG = 32, 64, 16
L = 8
NC = SEQ // L
TAPS = 31
PAD = TAPS - 1
ARUN = PAD + SEQ
SRUN = PAD + NT
AIN = ARUN + NB * SRUN
HEADS = 4
MEM = 256
PH = 8
TOPK = 16
TILES = SEQ // P
RMS_EPS, LN_EPS = 1e-6, 1e-5
PI = 3.141592653589793
TWO_PI_HI = 6.28125
TWO_PI_LO = 2 * PI - TWO_PI_HI
NEG = -3.0e38
RING = 8

COLS, _at = {}, 0
for _name, _n in (("b_in", 40), ("g1", 8), ("gm", 8), ("g2", 8), ("glu_b", 4), ("cw", 4 * TAPS),
                  ("cb", 4), ("lg", 4), ("lb", 4), ("d", G), ("keys", 256)):
    COLS[_name] = (_at, _n)
    _at += _n
N_CONST = _at
N_S5 = 3 * G + 4 * G * CG

JOBS = (["ssm", "ssx"] + [f"k{c}" for c in range(4)] + ["v"]
        + [f"{a}{c}" for c in range(4) for a in ("ag", "ai")]
        + [f"u{c}" for c in range(4)]
        + [f"{a}{b}" for b in range(4) for a in ("T", "ET")]
        + [f"z{e}{h}" for e in range(2) for h in range(2)]
        + [f"q{c}" for c in range(4)]
        + ["as0", "as1", "at0", "ao0", "as2", "at1", "ao1", "as3", "at2", "ao2", "at3", "ao3"]
        + ["ss_s", "ss_t", "ss_p", "ss_o"]
        + ["y0", "y1", "ys", "zs", "lnm", "lnv"]
        + [f"glu{c}" for c in range(4)])
LOOP_JOBS = 12
JOB_NUMBER = {n: i for i, n in enumerate(JOBS)}
GATE0 = len(JOBS)
_after = _after_jobs = GATE0 + 4 * LOOP_JOBS
TAIL = [f"o{c}" for c in range(8)] + ["ss2"] + [f"{a}{t}" for t in range(5) for a in ("xt", "ht")]
for _i, _n in enumerate(TAIL):
    JOB_NUMBER[_n] = _after + _i
JOB = {n: (i % 4, i // 4) for n, i in JOB_NUMBER.items()}
ROUTE0 = _after + len(TAIL)

LOADS = ([f"k{c}" for c in range(4)] + [f"v{c}" for c in range(4)]
         + [f"{a}{c}" for c in range(4) for a in ("ag", "ai")]
         + [f"u{c}" for c in range(4)] + [f"q{c}" for c in range(4)] + [f"glu{c}" for c in range(4)])
WS = 6
LOAD = {n: (i % WS, i // WS) for i, n in enumerate(LOADS)}
WGATE0 = len(LOADS)
_after = WGATE0 + 48
for _c in range(8):
    LOAD[f"o{_c}"] = ((_after + _c) % WS, (_after + _c) // WS)
WROUTE0 = _after + 8
LOADED_BEFORE = {n: JOB_NUMBER["v" if LOADS[i - WS][0] == "v" else LOADS[i - WS]]
                 for i, n in enumerate(LOADS) if i >= WS}
for _c in range(8):
    LOADED_BEFORE[f"o{_c}"] = _after_jobs - 6 + _c if _c < 6 else JOB_NUMBER[f"o{_c - 6}"]


def hybrid_step(nc, a, o):
    ctx = ExitStack()
    with ctx:
        def sem(name):
            return ctx.enter_context(nc.semaphore(name))

        arena = ctx.enter_context(nc.sbuf_tensor("arena", [P, 52992], F32))
        pairs = [ctx.enter_context(nc.psum_tensor(f"pair{i}", [P, 2, 512], F32)) for i in range(4)]
        ubuf = nc.dram_tensor("ubuf", [G * CG, TOK], F32, kind="Internal").ap()
        ybuf = nc.dram_tensor("ybuf", [G * CG, TOK], F32, kind="Internal").ap()

        def at(start, *shape):
            n = 1
            for x in shape:
                n *= x
            v = arena[:, start:start + n]
            names = "abcd"[:len(shape)]
            if len(shape) > 1:
                v = v.rearrange(f"p ({' '.join(names)}) -> p {' '.join(names)}",
                                **{x: s for x, s in zip(names[1:], shape[1:])})
            return v

        wring = at(0, WS, 1024)
        nT = at(6144, KD, TOK)
        R = 10496
        Tm = at(R, G, P)
        zz = at(R, HALF, TOK)
        ET = at(R + 4096, G, 192)
        xsq = at(R + 4096, KD, TOK)
        merged = at(R + 4096, KD, TOK)
        CL = at(R + 10240, G, L, CG)
        zg = at(R + 10240, HALF, TOK)
        Epad = at(R + 14336, G, 15, CG)
        Z = at(R + 14336, 2, G, NC + 1)
        Y = at(R + 14336 + 4160, G, NC)
        Ys = at(R + 14336 + 4160 + 2048, G, NB)
        h2T = at(R + 14336, KD, TOK)
        U = at(R + 22016, G, NC)
        Us = at(R + 24064, G, NB)
        Us2 = at(R + 24320, G, NB)
        tab = R + 22016
        ain = at(R + 24576, HALF, AIN)
        memT = at(R + 24576, KD, MEM)
        cact = at(R + 27832, HALF, TOK)
        msq = at(R + 27832, KD, MEM)
        qT = at(R + 30008, HALF, TOK)
        kT = at(R + 32184, HEADS, MEM)
        vm = at(R + 33208, 2, 512)
        Pm = at(R + 34232, HEADS, MEM)
        PT = at(R + 35256, HEADS, 2, P)
        sg = at(R + 34232, 2, TOK)
        xr = at(R + 35328, TOK)
        mr = at(R + 35328 + TOK, MEM)
        ut = at(R + 27832, HALF, TOK)
        gsg = at(R + 32184, 2, 3, TOK)
        gtmp = at(R + 32184 + 6 * TOK, TOK)
        lsq = at(R + 24576, HALF, TOK)
        lrs = at(R + 24576 + HALF * TOK, TOK)
        cring = at(R + 36280, 3, 1024)
        s5p = at(R + 36280, N_S5)
        h0 = at(R + 39352, 2, G, NB)
        ST = at(R + 39864, 2, P)
        Ps = at(R + 40120, MEM)
        PTs = at(R + 40376, 2, P)
        C0 = R + 40632
        const = at(C0, N_CONST)
        ident = at(C0 + N_CONST, P)
        ones = at(C0 + N_CONST + P, P)
        SM = C0 + N_CONST + 2 * P
        mx, nmx, asum, ars = (at(SM + 4 * i, 4) for i in range(4))
        sgn = at(SM + 16, 1)
        A8 = at(SM + 20, 2, G)
        B8 = at(SM + 84, 2, G)
        A4 = at(SM + 148, G)
        B4 = at(SM + 180, G)
        dve_t = at(SM + 212, 2, 64)
        xbT = at(6144, KD, 5 * P)
        h2 = at(11264, 5, D)
        uring = at(16384, RING, D)
        vring = at(24576, RING, D)
        h2sq = at(29184, KD, TOK)
        h2r = at(33536, TOK)
        diag = at(32768, RING, P)
        sw = at(33792, 2, P)
        sc = at(34080, 5 * PH, 2, P)
        xb = at(44320, 5, D)
        expert = at(49440, 5 * PH, TOPK).bitcast(U32)
        gate = at(50080, 5 * PH, TOPK)
        Q0 = 50720
        dots = at(Q0, 2, TOPK)
        gel = at(Q0 + 32, 2, TOPK)
        idx_u = at(Q0 + 64, 2, TOPK).bitcast(U32)
        idx_v = at(Q0 + 96, 2, TOPK).bitcast(U32)
        idx_s = at(Q0 + 128, 32).bitcast(U32)
        gate_s = at(Q0 + 160, 32)
        fold = at(Q0 + 192, 32)
        esum, ers = at(Q0 + 224, 1), at(Q0 + 225, 1)
        fss, frs = at(Q0 + 226, 1), at(Q0 + 227, 1)
        iota16 = at(Q0 + 228, TOPK)
        qbuf = at(4096, 2, 5 * P)
        cand = at(5376, 16, 16)
        eq = at(5632, 16, 16)
        tv = at(5888, 2, TOPK)
        tif = at(5920, 2, TOPK)
        tiu = at(5952, 2, TOPK).bitcast(U32)
        cv = at(5984, TOPK)
        ciu = at(6000, TOPK).bitcast(U32)
        hlu = at(6016, 2, TOPK).bitcast(U32)
        hlf = at(6048, 2, TOPK)
        i12 = at(6080, 2, TOPK)
        ce = at(6112, TOPK)
        xbcur = at(6144, D)
        acc = at(7168, D)
        ytile = at(8192, D)
        gf = at(9216, D)

        def c(name, i=0, n=1):
            s = COLS[name][0] + i
            return const[:, s:s + n]

        consts_in, s5_in, x_in, mem_in, h0_in = (sem(n) for n in ("consts_in", "s5_in", "x_in", "mem_in", "h0_in"))
        w_in = [sem(f"w_in{i}") for i in range(WS)]
        full = [sem(f"full{i}") for i in range(4)]
        free = [sem(f"free{i}") for i in range(4)]
        made = sem("made")
        pool_step, dve_step, conv_step, scan_step, route_step = (sem(n) for n in (
            "pool_step", "dve_step", "conv_step", "scan_step", "route_step"))
        msq_ok, xsq_ok, rms_ok, m_ok, n_ok = (sem(n) for n in ("msq_ok", "xsq_ok", "rms_ok", "m_ok", "n_ok"))
        epad_ok, s5_scan_in = sem("epad_ok"), sem("s5_functions_ok")
        ain_zero, ain_ok, conv_out, mem_out, state_out = (sem(n) for n in (
            "ain_history_in", "ain_ok", "conv_out", "mem_out", "state_out"))
        us_zero, ubuf_ok, u_ok, scan_ok, ybuf_ok, y_in = (sem(n) for n in (
            "us_zero", "ubuf_ok", "u_in_chunks", "scan_ok", "ybuf_ok", "y_in"))
        max_ok, p_ok = sem("max_ok"), sem("p_ok")
        cin = [sem(f"cache_in{i}") for i in range(3)]
        c_used = [sem(f"cache_used{i}") for i in range(3)]
        zz_ok, zg_ok, lnx_ok, lsq_ok, lr_ok, cact_ok = (sem(n) for n in (
            "zz_ok", "zg_ok", "lnx_ok", "lsq_ok", "lr_ok", "cact_ok"))
        merged_ok, x2_in, h2sq_ok, h2r_ok, xbT_ok, gf_in, iota_ok = (sem(n) for n in (
            "merged_ok", "x2_in", "h2sq_ok", "h2r_ok", "xbT_ok", "gf_in", "iota_ok"))
        routed, cdiff, cexp, xload = (sem(n) for n in ("routed", "cdiff", "cexp", "xload"))
        u_in = [sem(f"u_in{i}") for i in range(RING)]
        v_in = [sem(f"v_in{i}") for i in range(RING)]
        u_used, v_used, gel_ok, w_ok, idxv_ok, diag_ok = (sem(n) for n in (
            "u_used", "v_used", "gel_ok", "w_ok", "idxv_ok", "diag_ok"))
        slot_free = sem("slot_free")
        acc_step, acc_ok, fsq_ok, fms_ok, frt_ok, yt_ok, yt_out = (sem(n) for n in (
            "acc_step", "acc_ok", "fsq_ok", "fms_ok", "frt_ok", "yt_ok", "yt_out"))

        block = ctx.enter_context(nc.Block())

        def pair(name):
            return pairs[JOB[name][0]]

        def filled(eng, name):
            p, n = JOB[name]
            eng.wait_ge(full[p], n + 1)
            return pairs[p]

        def emptied(eng, name):
            p, n = JOB[name]
            eng.wait_ge(free[p], n + 1)

        def drained(name):
            return free[JOB[name][0]]

        def flat(p, n=TOK):
            return p.rearrange("p a b -> p (a b)")[:, 0:n]

        def two(p):
            return p[:, :, 0:HT]

        def halves(v):
            return v.rearrange("p (a b) -> p a b", a=2)

        def utq(j):
            v = ut[:, j, :]
            return (v[:, 0:SEQ].rearrange("p (j c) -> p j c", j=L),
                    v[:, SEQ:].rearrange("p (t b) -> p t b", t=NT))

        def finish_act(act, t, rows):
            act.wait_ge(acc_ok, t + 1)
            if t:
                act.wait_ge(yt_out, 16 * t)
            act.activation(ytile[0:rows, :], acc[0:rows, :], ACT.Square, accum_out=fss[0:rows, :]).then_inc(fsq_ok, 1)
            act.wait_ge(fms_ok, t + 1)
            act.activation(frs[0:rows, :], frs[0:rows, :], ACT.Sqrt).then_inc(frt_ok, 1)

        @block.sync
        def _(sp):
            sp.dma_start(s5p, a["s5_pack"]).then_inc(s5_in, 16)
            sp.dma_start(memT, a["mem_t"]).then_inc(mem_in, 16)
            sp.dma_start(const, a["consts"]).then_inc(consts_in, 16)
            sp.dma_start(nT, a["x_t"]).then_inc(x_in, 16)

            def load(name, src, k=KD):
                s, n = LOAD[name]
                if n:
                    before = LOADED_BEFORE[name]
                    sp.wait_ge(full[before % 4], before // 4 + 1)
                sp.dma_start(wring[:, s, 0:k * P], src).then_inc(w_in[s], 16)

            for j in range(4):
                load(f"k{j}", a["w_mem_k"][j])
            for j in range(4):
                load(f"v{j}", a["w_mem_v"][j])
            sp.dma_start(h0.rearrange("p a b c -> p (a b c)"), a["h0"]).then_inc(h0_in, 16)
            for j in range(4):
                load(f"ag{j}", a["w_in"][8 + j])
                load(f"ai{j}", a["w_in"][4 + j])
            for j in range(4):
                load(f"u{j}", a["w_in"][j])
            for j in range(4):
                load(f"q{j}", a["w_in"][12 + j])
            filled(sp, "T3")
            for n in range(2 * NB):
                if n >= 3:
                    sp.wait_ge(c_used[n % 3], n // 3)
                src = a["cache_k"][n] if n < NB else a["cache_v"][n - NB]
                sp.dma_start(cring[:, n % 3, :], src).then_inc(cin[n % 3], 16)
            for j in range(4):
                load(f"glu{j}", a["glu_w"][j], HALF)
            with sp.Fori(0, 4) as i:
                for r in range(2):
                    for b in range(6):
                        n = WGATE0 + 6 * r + b
                        s = n % WS
                        job = GATE0 + 6 * r + b - 6
                        sp.wait_ge(full[job % 4], job // 4 + 1 + 3 * i)
                        if b < 3:
                            sp.dma_start(wring[:, s, :], a["w_in"][bass.ds(16 + 8 * b + r + 2 * i, 1)]
                                         .rearrange("a p n -> (a p) n")).then_inc(w_in[s], 16)
                        else:
                            sp.dma_start(wring[:, s, 0:512], a["proj"][b - 3][bass.ds(r + 2 * i, 1)]
                                         .rearrange("a p n -> (a p) n")).then_inc(w_in[s], 16)
            for j in range(8):
                load(f"o{j}", a["w_out"][j])
                if j == 3:
                    sp.wait_ge(zz_ok, 4)
                    sp.wait_ge(state_out, 32)
                    sp.dma_start(h2T, a["x_t"]).then_inc(x2_in, 16)
            for b in range(4):
                before = JOB_NUMBER[f"o{b + 2}"]
                sp.wait_ge(full[before % 4], before // 4 + 1)
                sp.dma_start(wring[:, b, :], a["peer_q"][b]).then_inc(w_in[b], 16)
            with sp.Fori(1, 4) as i:
                for b in range(4):
                    job = ROUTE0 + 4 * (b // 2) + b % 2 - 8
                    sp.wait_ge(full[job % 4], job // 4 + 1 + 2 * i)
                    sp.dma_start(wring[:, b, :], a["peer_q"][bass.ds(4 * i + b, 1)]
                                 .rearrange("a p n -> (a p) n")).then_inc(w_in[b], 16)
            job = ROUTE0 + 31
            sp.wait_ge(full[job % 4], job // 4 + 1)
            sp.dma_start(gf, a["final_g"].partition_broadcast(P)).then_inc(gf_in, 16)
            for t in range(TILES + 1):
                sp.wait_ge(yt_ok, t + 1)
                rows = P if t < TILES else NB * NT
                sp.dma_start(o["y"][t * P:t * P + rows, :], ytile[0:rows, :]).then_inc(yt_out, 16)
            sp.wait_ge(yt_out, 16 * (TILES + 1))
            sp.wait_ge(conv_out, 16 * (1 + HALF))
            sp.wait_ge(mem_out, 32)
            sp.wait_ge(state_out, 32)

        def loads_before_route(s):
            return (WROUTE0 - s + WS - 1) // WS

        @block.gpsimd
        def _(pool):
            pool.memset(ident, 0.0).then_inc(pool_step, 1)
            pool.wait_ge(pool_step, 1)
            pool.affine_select(out=ident, in_=ident, compare_op=ALU.not_equal, fill=1.0, base=0,
                               pattern=[[-1, P]], channel_multiplier=1).then_inc(made, 1)
            pool.memset(ones, 1.0).then_inc(made, 1)
            filled(pool, "v")
            for j in range(HALF):
                pool.memset(ain[:, j, 0:PAD], 0.0).then_inc(pool_step, 1)
            hist = ain[:, :, ARUN:].rearrange("p c (b k) -> p c b k", b=NB)
            for j in range(HALF):
                pool.dma_start(hist[:, j, :, 0:PAD], a["conv_hist"][:, j]).then_inc(ain_zero, 16)
            pool.wait_ge(pool_step, 1 + HALF)
            pool.wait_ge(ain_zero, 16 * HALF)
            for j in range(HALF):
                emptied(pool, f"ai{j}")
                pool.tensor_tensor(ain[:, j, PAD:ARUN], ain[:, j, PAD:ARUN], sg[:, j % 2, 0:SEQ], ALU.mult)
                pool.tensor_tensor(hist[:, j, :, PAD:], hist[:, j, :, PAD:],
                                   sg[:, j % 2, SEQ:].rearrange("p (b t) -> p b t", b=NB),
                                   ALU.mult).then_inc(ain_ok, 1)
            pool.wait_ge(ain_ok, HALF)
            pool.dma_start(o["conv_p"], ain[:, :, SEQ:ARUN]).then_inc(conv_out, 16)
            for j in range(HALF):
                pool.dma_start(o["conv_s"][:, j], hist[:, j, :, NT:]).then_inc(conv_out, 16)
            emptied(pool, "u3")
            pool.dma_start(ubuf.rearrange("(q p) t -> p q t", p=P), ut).then_inc(ubuf_ok, 16)
            pool.wait_ge(epad_ok, 2)
            pool.memset(Us, 0.0).then_inc(us_zero, 1)
            pool.memset(Us2, 0.0).then_inc(us_zero, 1)
            pool.wait_ge(ubuf_ok, 16)
            pool.wait_ge(us_zero, 2)
            src = ubuf.rearrange("(g i) t -> i g t", i=CG)
            for j in range(L):
                pool.dma_start(U[CG * j:CG * (j + 1), :, :], src[:, :, NC * j:NC * (j + 1)]).then_inc(u_ok, 16)
            for j in range(NT):
                part = src[:, :, SEQ + NB * j:SEQ + NB * (j + 1)]
                pool.dma_start(Us[CG * j:CG * (j + 1), :, :], part).then_inc(u_ok, 16)
                pool.dma_start(Us2[64 + CG * j:64 + CG * (j + 1), :, :], part).then_inc(u_ok, 16)
            for n in ("k0", "k1", "k2", "k3", "v"):
                emptied(pool, n)
            pool.dma_start(o["mem_k"], kT).then_inc(mem_out, 16)
            pool.dma_start(o["mem_v"], vm).then_inc(mem_out, 16)
            for n in ("y0", "y1", "ys"):
                emptied(pool, n)
            dst = ybuf.rearrange("(g i) t -> i g t", i=CG)
            for j in range(L):
                pool.dma_start(dst[:, :, NC * j:NC * (j + 1)], Y[CG * j:CG * (j + 1), :, :]).then_inc(ybuf_ok, 16)
            for j in range(NT):
                pool.dma_start(dst[:, :, SEQ + NB * j:SEQ + NB * (j + 1)],
                               Ys[CG * j:CG * (j + 1), :, :]).then_inc(ybuf_ok, 16)
            pool.wait_ge(ybuf_ok, 16 * (L + NT))
            pool.dma_start(zg, ybuf.rearrange("(q p) t -> p q t", p=P)).then_inc(y_in, 16)
            pool.wait_ge(scan_ok, 1)
            pool.dma_start(o["ssm_p"], dve_t[:, 0, 0:G]).then_inc(state_out, 16)
            emptied(pool, "zs")
            pool.dma_start(o["ssm_s"], h0[:, 0]).then_inc(state_out, 16)
            pool.iota(iota16.bitcast(I32), pattern=[[1, TOPK]], base=0, channel_multiplier=0).then_inc(iota_ok, 1)

            def gather_u(n, par):
                pool.wait_ge(routed, n + 1)
                for j in range(TOPK):
                    first = isinstance(n, int) and n == 0 and j < RING
                    if not first:
                        pool.wait_ge(u_used, TOPK * n + (j - RING + 1))
                        pool.sem_inc(slot_free, 1)
                    pool.indirect_dma_start(uring[:, j % RING, :], None, a["peer_u"],
                                            bass.IndirectOffsetOnAxis(ap=idx_u[:, par, j:j + 1], axis=0)
                                            ).then_inc(u_in[j % RING], 16)

            def gather_v(n, par):
                pool.wait_ge(idxv_ok, n + 1)
                for j in range(TOPK):
                    first = isinstance(n, int) and n == 0 and j < RING
                    if not first:
                        pool.wait_ge(v_used, TOPK * n + (j - RING + 1))
                        pool.sem_inc(slot_free, 1)
                    pool.indirect_dma_start(vring[:, j % RING, :], None, a["peer_v"],
                                            bass.IndirectOffsetOnAxis(ap=idx_v[:, par, j:j + 1], axis=0)
                                            ).then_inc(v_in[j % RING], 16)

            gather_u(0, 0)
            gather_u(1, 1)
            with pool.Fori(1, 4) as i:
                gather_u(2 * i, 0)
                gather_u(2 * i + 1, 1)
            gather_u(8, 0)
            gather_v(0, 0)
            gather_u(9, 1)
            gather_v(1, 1)
            with pool.Fori(5, 16) as i:
                gather_u(2 * i, 0)
                gather_v(2 * i - PH, 0)
                gather_u(2 * i + 1, 1)
                gather_v(2 * i + 1 - PH, 1)
            with pool.Fori(12, 16) as i:
                gather_v(2 * i, 0)
                gather_v(2 * i + 1, 1)
            n = TOPK * TILES * PH
            pool.wait_ge(routed, TILES * PH + 3)
            for j in range(32):
                pool.wait_ge(u_used, n + j - RING + 1)
                pool.indirect_dma_start(uring[:, j % RING, :], None, a["peer_u"],
                                        bass.IndirectOffsetOnAxis(ap=idx_s[:, j:j + 1], axis=0)
                                        ).then_inc(u_in[j % RING], 16)
            for j in range(32):
                pool.wait_ge(v_used, n + j - RING + 1)
                pool.indirect_dma_start(vring[:, j % RING, :], None, a["peer_v"],
                                        bass.IndirectOffsetOnAxis(ap=idx_s[:, j:j + 1], axis=0)
                                        ).then_inc(v_in[j % RING], 16)

        @block.tensor
        def _(pe):
            def begin(name):
                p, n = JOB[name]
                if n:
                    pe.wait_ge(free[p], n)
                return pairs[p]

            def loaded(name):
                s, n = LOAD[name]
                pe.wait_ge(w_in[s], 16 * (n + 1))
                return wring[:, s, :].rearrange("p (k m) -> p k m", m=P)

            def product(ps, w, rhs, k, step=True):
                for j in range(k):
                    for h in range(2):
                        mm = pe.matmul(ps[:, h, 0:HT], w[:, j, :], rhs[:, j, h * HT:(h + 1) * HT],
                                       start=(j == 0), stop=(j == k - 1))
                return mm

            def weighted(name, rhs, k=KD):
                w = loaded(name)
                ps = begin(name)
                product(ps, w, rhs, k).then_inc(full[JOB[name][0]], 1)

            pe.wait_ge(made, 2)
            ps = begin("ssm")
            for k in range(KD):
                pe.wait_ge(msq_ok, k + 1)
                mm = pe.matmul(ps[:, 0, 0:MEM], ones, msq[:, k, :], start=(k == 0), stop=(k == KD - 1))
            mm.then_inc(full[0], 1)
            ps = begin("ssx")
            for k in range(KD):
                pe.wait_ge(xsq_ok, k + 1)
                for h in range(2):
                    mm = pe.matmul(ps[:, h, 0:HT], ones, xsq[:, k, h * HT:(h + 1) * HT],
                                   start=(k == 0), stop=(k == KD - 1))
            mm.then_inc(full[1], 1)
            pe.wait_ge(m_ok, KD)
            for j in range(4):
                w = loaded(f"k{j}")
                ps = begin(f"k{j}")
                for k in range(KD):
                    mm = pe.matmul(ps[:, 0, 0:MEM], w[:, k, :], memT[:, k, :], start=(k == 0), stop=(k == KD - 1))
                mm.then_inc(full[JOB[f"k{j}"][0]], 1)
            ps = begin("v")
            for j in range(4):
                w = loaded(f"v{j}")
                for m in range(2):
                    for k in range(KD):
                        mm = pe.matmul(ps[:, m, j * P:(j + 1) * P], memT[:, k, m * P:(m + 1) * P], w[:, k, :],
                                       start=(k == 0), stop=(k == KD - 1))
            mm.then_inc(full[JOB["v"][0]], 1)
            pe.wait_ge(n_ok, KD)
            for j in range(4):
                weighted(f"ag{j}", nT)
                weighted(f"ai{j}", nT)
            for j in range(4):
                weighted(f"u{j}", nT)
            s5C = s5p[:, 3 * G + 2 * G * CG:3 * G + 3 * G * CG].rearrange("p (g i) -> p g i", g=G)
            pe.wait_ge(epad_ok, 2)
            for b in range(4):
                ps = flat(begin(f"T{b}"), 1024).rearrange("p (g i o) -> p g i o", g=8, i=L)
                for g in range(8):
                    for i in range(L):
                        mm = pe.matmul(ps[:, g, i, :], Epad[:, 8 * b + g, L - 1 - i:2 * L - 1 - i, :],
                                       s5C[:, 8 * b + g, :], start=True, stop=True)
                mm.then_inc(full[JOB[f"T{b}"][0]], 1)
                ps = flat(begin(f"ET{b}"), 1024).rearrange("p (g n) -> p g n", g=8)
                for g in range(8):
                    mm = pe.transpose(ps[:, g, :], Epad[:, 8 * b + g, 0:L, :].rearrange("p s i -> p (s i)"), ident)
                mm.then_inc(full[JOB[f"ET{b}"][0]], 1)
            pe.wait_ge(u_ok, 16 * (L + 2 * NT))
            for b in range(4):
                emptied(pe, f"ET{b}")
            for e in range(2):
                for h in range(2):
                    ps = flat(begin(f"z{e}{h}"), 1024).rearrange("p (g n) -> p g n", g=16)
                    for g in range(16):
                        mm = pe.matmul(ps[:, g, :], ET[:, 16 * h + g, 64 * e:64 * e + P], U[:, 16 * h + g, :],
                                       start=True, stop=True)
                    mm.then_inc(full[JOB[f"z{e}{h}"][0]], 1)
            for j in range(4):
                weighted(f"q{j}", nT)

            def scores(t):
                if t == 0:
                    for n in ("q0", "q1", "q2", "q3", "k0", "k1", "k2", "k3", "v"):
                        emptied(pe, n)
                ps = flat(begin(f"as{t}"), 1024).rearrange("p (h m) -> p h m", h=HEADS)
                for h in range(HEADS):
                    mm = pe.matmul(ps[:, h, :], qT[:, h, t * P:(t + 1) * P], kT[:, h, :], start=True, stop=True)
                mm.then_inc(full[JOB[f"as{t}"][0]], 1)

            def turn(t):
                pe.wait_ge(p_ok, t + 1)
                ps = flat(begin(f"at{t}"), 1024).rearrange("p (h c m) -> p h c m", h=HEADS, c=2)
                for h in range(HEADS):
                    for m in range(2):
                        mm = pe.transpose(ps[:, h, m, :], Pm[:, h, m * P:(m + 1) * P], ident)
                mm.then_inc(full[JOB[f"at{t}"][0]], 1)

            def values(t):
                emptied(pe, f"at{t}")
                ps = begin(f"ao{t}")
                for h in range(HEADS):
                    for m in range(2):
                        mm = pe.matmul(ps[:, 0, h * P:(h + 1) * P], vm[:, m, h * P:(h + 1) * P], PT[:, h, m, :],
                                       start=(m == 0), stop=(m == 1))
                mm.then_inc(full[JOB[f"ao{t}"][0]], 1)

            scores(0)
            for t in range(TILES):
                if t + 1 < TILES:
                    scores(t + 1)
                turn(t)
                values(t)
            ps = begin("ss_s")
            for b in range(NB):
                pe.wait_ge(cin[b % 3], 16 * (b // 3 + 1))
                kc = cring[:, b % 3, :].rearrange("p (h m) -> p h m", h=HEADS)
                for h in range(HEADS):
                    for m in range(2):
                        mm = pe.matmul(ps[:, 0, m * P + 16 * b + 4 * h:m * P + 16 * b + 4 * h + NT],
                                       kc[:, h, m * P:(m + 1) * P], qT[:, h, SEQ + NT * b:SEQ + NT * (b + 1)],
                                       start=True, stop=True)
                if b < NB - 1:
                    mm.then_inc(c_used[b % 3], 1)
            mm.then_inc(full[JOB["ss_s"][0]], 1)
            pe.wait_ge(full[JOB["ss_s"][0]], JOB["ss_s"][1] + 1)
            pe.sem_inc(c_used[(NB - 1) % 3], 1)
            ps = begin("ss_t")
            emptied(pe, "ss_s")
            for m in range(2):
                mm = pe.transpose(ps[:, 0, m * P:(m + 1) * P], ST[:, m, :], ident)
            mm.then_inc(full[JOB["ss_t"][0]], 1)
            ps = begin("ss_p")
            pe.wait_ge(p_ok, TILES + 1)
            for m in range(2):
                mm = pe.transpose(ps[:, 0, m * P:(m + 1) * P], Ps[:, m * P:(m + 1) * P], ident)
            mm.then_inc(full[JOB["ss_p"][0]], 1)
            ps = begin("ss_o")
            emptied(pe, "ss_p")
            for b in range(NB):
                n = NB + b
                pe.wait_ge(cin[n % 3], 16 * (n // 3 + 1))
                vc = cring[:, n % 3, :].rearrange("p (c n) -> p c n", c=2)
                for h in range(HEADS):
                    for m in range(2):
                        mm = pe.matmul(ps[:, 0, 32 * h + NT * b:32 * h + NT * (b + 1)], vc[:, m, h * P:(h + 1) * P],
                                       PTs[:, m, 16 * b + 4 * h:16 * b + 4 * h + NT],
                                       start=(m == 0), stop=(m == 1))
                if b < NB - 1:
                    mm.then_inc(c_used[n % 3], 1)
            mm.then_inc(full[JOB["ss_o"][0]], 1)
            pe.wait_ge(scan_ok, 1)
            for b in range(4):
                emptied(pe, f"T{b}")
            for h in range(2):
                ps = flat(begin(f"y{h}"), 1024).rearrange("p (g n) -> p g n", g=16)
                for g in range(16):
                    gg = 16 * h + g
                    pe.matmul(ps[:, g, :], Tm[:, gg, :], U[:, gg, :], start=True, stop=False)
                    mm = pe.matmul(ps[:, g, :], CL[:, gg, :, :].rearrange("p i o -> p (i o)"), Z[:, 0, gg, 0:NC],
                                   start=False, stop=True)
                mm.then_inc(full[JOB[f"y{h}"][0]], 1)
            ps = begin("ys")
            pe.wait_ge(h0_in, 16)
            for g in range(G):
                pe.matmul(ps[:, 0, NB * g:NB * (g + 1)], Tm[:, g, :], Us[:, g, :], start=True, stop=False)
                mm = pe.matmul(ps[:, 0, NB * g:NB * (g + 1)], CL[:, g, :, :].rearrange("p i o -> p (i o)"),
                               h0[:, 0, g, :], start=False, stop=True)
            mm.then_inc(full[JOB["ys"][0]], 1)
            ps = begin("zs")
            for g in range(G):
                mm = pe.matmul(ps[:, 0, NB * g:NB * (g + 1)], ET[:, g, 0:P], Us2[:, g, :], start=True, stop=True)
            mm.then_inc(full[JOB["zs"][0]], 1)
            for name, src, ready in (("lnm", cact, None), ("lnv", lsq, lsq_ok)):
                ps = begin(name)
                if ready is None:
                    pe.wait_ge(conv_step, 2 * TAPS * HALF)
                for k in range(HALF):
                    if ready is not None:
                        pe.wait_ge(ready, k + 1)
                    for h in range(2):
                        mm = pe.matmul(ps[:, h, 0:HT], ones, src[:, k, h * HT:(h + 1) * HT],
                                       start=(k == 0), stop=(k == HALF - 1))
                mm.then_inc(full[JOB[name][0]], 1)
            pe.wait_ge(zz_ok, HALF)
            for j in range(4):
                weighted(f"glu{j}", zz, HALF)
            emptied(pe, "ao3")
            emptied(pe, "ss_o")
            pe.wait_ge(zg_ok, HALF)
            pe.wait_ge(cact_ok, HALF)
            with pe.Fori(0, 4) as i:
                for r in range(2):
                    for b in range(6):
                        job, ld = GATE0 + 6 * r + b, WGATE0 + 6 * r + b
                        p, s = job % 4, ld % WS
                        pe.wait_ge(w_in[s], 16 * (ld // WS + 1) + 32 * i)
                        pe.wait_ge(free[p], job // 4 + 3 * i)
                        w = wring[:, s, :].rearrange("p (k m) -> p k m", m=P)
                        mm = product(pairs[p], w, nT if b < 3 else (zg, cact, qT)[b - 3], KD if b < 3 else HALF)
                        mm.then_inc(full[p], 1)
            pe.wait_ge(merged_ok, 2 * KD)
            for j in range(8):
                weighted(f"o{j}", merged)
            ps = begin("ss2")
            for k in range(KD):
                pe.wait_ge(h2sq_ok, k + 1)
                for h in range(2):
                    mm = pe.matmul(ps[:, h, 0:HT], ones, h2sq[:, k, h * HT:(h + 1) * HT],
                                   start=(k == 0), stop=(k == KD - 1))
            mm.then_inc(full[JOB["ss2"][0]], 1)
            pe.wait_ge(xbT_ok, KD)
            for t in range(TILES + 1):
                ps = flat(begin(f"xt{t}"), 1024)
                for k in range(KD):
                    mm = pe.transpose(ps[:, k * P:(k + 1) * P], xbT[:, k, t * P:(t + 1) * P], ident)
                mm.then_inc(full[JOB[f"xt{t}"][0]], 1)
                ps = flat(begin(f"ht{t}"), 1024)
                rows = P if t < TILES else NB * NT
                for k in range(KD):
                    mm = pe.transpose(ps[0:rows, k * P:(k + 1) * P], h2T[:, k, t * P:t * P + rows], ident)
                mm.then_inc(full[JOB[f"ht{t}"][0]], 1)
            keys = c("keys", 0, 256).rearrange("p (s k) -> p s k", s=2)
            with pe.Fori(0, 4) as i:
                for r in range(2):
                    for b in range(4):
                        job = ROUTE0 + 4 * r + b
                        p = job % 4
                        pe.wait_ge(free[p], job // 4 + 2 * i)
                        if b < 2:
                            s = 2 * r + b
                            pe.wait_ge(w_in[s], 16 * (loads_before_route(s) + 1) + 16 * i)
                            w = wring[:, s, :].rearrange("p (k m) -> p k m", m=P)
                            mm = product(pairs[p], w, xbT, KD)
                            mm.then_inc(full[p], 1)
                        else:
                            qj = job - 2
                            pe.wait_ge(free[qj % 4], qj // 4 + 1 + 2 * i)
                            for t in range(TILES + 1):
                                mm = pe.matmul(flat(pairs[p], 640)[:, t * P:(t + 1) * P],
                                               qbuf[:, b - 2, t * P:(t + 1) * P], keys[:, b - 2, :],
                                               start=True, stop=True)
                            mm.then_inc(full[p], 1)

            def sum_v(n, par):
                if not (isinstance(n, int) and n < 2):
                    pe.wait_ge(acc_step, n)
                for j in range(TOPK):
                    pe.wait_ge(v_in[j % RING], 32 * n + 16 * (j // RING + 1))
                    pe.wait_ge(diag_ok, TOPK * n + j + 1)
                    for h in range(2):
                        mm = pe.matmul(pairs[par][:, h, :], diag[:, j % RING, :],
                                       vring[:, j % RING, h * 512:(h + 1) * 512],
                                       start=(j == 0), stop=(j == TOPK - 1))
                    mm.then_inc(v_used, 1)

            for p in range(4):
                pe.wait_ge(free[p], (ROUTE0 + 32 - p + 3) // 4)
            sum_v(0, 0)
            sum_v(1, 1)
            with pe.Fori(1, 16) as i:
                sum_v(2 * i, 0)
                sum_v(2 * i + 1, 1)
            n = TOPK * TILES * PH
            pe.wait_ge(acc_step, TILES * PH)
            for j in range(32):
                pe.wait_ge(v_in[j % RING], 16 * (2 * TILES * PH + j // RING + 1))
                pe.wait_ge(diag_ok, n + j + 1)
                for h in range(2):
                    mm = pe.matmul(pairs[0][0:32, h, :], diag[:, j % RING, 0:32],
                                   vring[:, j % RING, h * 512:(h + 1) * 512], start=(j == 0), stop=(j == 31))
                mm.then_inc(v_used, 1)

        @block.scalar
        def _(act):
            act.wait_ge(mem_in, 16)
            for k in range(KD):
                act.activation(msq[:, k, :], memT[:, k, :], ACT.Square).then_inc(msq_ok, 1)
            act.wait_ge(x_in, 16)
            for k in range(KD):
                act.activation(xsq[:, k, :], nT[:, k, :], ACT.Square).then_inc(xsq_ok, 1)
            act.wait_ge(s5_in, 16)
            act.activation(at(tab, G), s5p[:, 0:G], ACT.Tanh, scale=1.0 / 16).then_inc(s5_scan_in, 1)
            act.wait_ge(epad_ok, 1)
            act.activation(at(tab + 288 * 2, 288), at(tab + 288 * 2, 288), ACT.Tanh, scale=0.5).then_inc(s5_scan_in, 1)
            act.activation(at(tab + 288 * 3, 288), at(tab, 288), ACT.Sin)
            act.activation(at(tab + 288 * 4, 288), at(tab + 288, 288), ACT.Sin)
            act.activation(at(tab + 2304, G), at(tab + 2304, G), ACT.Sin, scale=0.5).then_inc(s5_scan_in, 1)
            act.wait_ge(consts_in, 16)
            emptied(act, "ssm")
            act.activation(mr, mr, ACT.Sqrt).then_inc(rms_ok, 1)
            emptied(act, "ssx")
            act.activation(xr, xr, ACT.Sqrt).then_inc(rms_ok, 1)
            for j in range(4):
                ps = filled(act, f"k{j}")
                act.activation(kT[:, j, :], ps[:, 0, 0:MEM], ACT.Copy).then_inc(drained(f"k{j}"), 1)
            ps = filled(act, "v")
            act.activation(vm.rearrange("p a b -> p (a b)"), flat(ps, 1024), ACT.Copy).then_inc(drained("v"), 1)
            hist = ain[:, :, ARUN:].rearrange("p c (b k) -> p c b k", b=NB)
            for j in range(4):
                ps = filled(act, f"ag{j}")
                if j >= 2:
                    act.wait_ge(ain_ok, j - 1)
                act.activation(halves(sg[:, j % 2, :]), two(ps), ACT.Sigmoid, bias=c("b_in", 8 + j)
                               ).then_inc(drained(f"ag{j}"), 1)
                ps = filled(act, f"ai{j}")
                act.activation(ain[:, j, PAD:PAD + HT], ps[:, 0, 0:HT], ACT.Identity, bias=c("b_in", 4 + j))
                act.activation(ain[:, j, PAD + HT:ARUN], ps[:, 1, 0:SEQ - HT], ACT.Identity, bias=c("b_in", 4 + j))
                act.activation(hist[:, j, :, PAD:], ps[:, 1, SEQ - HT:HT].rearrange("p (b t) -> p b t", b=NB),
                               ACT.Identity, bias=c("b_in", 4 + j)).then_inc(drained(f"ai{j}"), 1)
            for j in range(4):
                ps = filled(act, f"u{j}")
                dst = utq(j)
                act.activation(dst[0][:, :, 0:HT // L], ps[:, 0, 0:HT].rearrange("p (c j) -> p j c", j=L),
                               ACT.Identity, bias=c("b_in", j))
                act.activation(dst[0][:, :, HT // L:NC], ps[:, 1, 0:SEQ - HT].rearrange("p (c j) -> p j c", j=L),
                               ACT.Identity, bias=c("b_in", j))
                act.activation(dst[1], ps[:, 1, SEQ - HT:HT].rearrange("p (b t) -> p t b", b=NB),
                               ACT.Identity, bias=c("b_in", j)).then_inc(drained(f"u{j}"), 1)
            for b in range(4):
                ps = flat(filled(act, f"T{b}"), 1024)
                act.activation(Tm[:, 8 * b:8 * b + 8, :].rearrange("p g n -> p (g n)"), ps, ACT.Copy
                               ).then_inc(drained(f"T{b}"), 1)
                ps = flat(filled(act, f"ET{b}"), 1024).rearrange("p (g n) -> p g n", g=8)
                act.activation(ET[:, 8 * b:8 * b + 8, 0:P], ps, ACT.Copy)
                act.activation(ET[:, 8 * b:8 * b + 8, P:], ps[:, :, 0:64], ACT.Copy).then_inc(drained(f"ET{b}"), 1)
            for e in range(2):
                for h in range(2):
                    ps = flat(filled(act, f"z{e}{h}"), 1024).rearrange("p (g n) -> p g n", g=16)
                    act.activation(Z[:, e, 16 * h:16 * h + 16, 1:], ps, ACT.Copy).then_inc(drained(f"z{e}{h}"), 1)
            for j in range(4):
                ps = filled(act, f"q{j}")
                act.activation(halves(qT[:, j, :]), two(ps), ACT.Identity, bias=c("b_in", 12 + j)
                               ).then_inc(drained(f"q{j}"), 1)
            scale = float(P) ** -0.5
            for t in range(TILES):
                ps = flat(filled(act, f"as{t}"), 1024).rearrange("p (h m) -> p h m", h=HEADS)
                act.wait_ge(max_ok, t + 1)
                for h in range(HEADS):
                    ins = act.activation(Pm[:, h, :], ps[:, h, :], ACT.Exp, bias=nmx[:, h:h + 1], scale=scale,
                                         accum_out=asum[:, h:h + 1])
                ins.then_inc(drained(f"as{t}"), 1)
                ps = filled(act, f"at{t}")
                act.activation(PT.rearrange("p h c m -> p (h c m)"), flat(ps, 1024), ACT.Copy
                               ).then_inc(drained(f"at{t}"), 1)
                ps = filled(act, f"ao{t}")
                act.activation(qT[:, :, t * P:(t + 1) * P], ps[:, 0, :].rearrange("p (h t) -> p h t", h=HEADS),
                               ACT.Copy).then_inc(drained(f"ao{t}"), 1)
            ps = filled(act, "ss_s")
            act.activation(ST.rearrange("p a b -> p (a b)"), ps[:, 0, 0:MEM], ACT.Copy).then_inc(drained("ss_s"), 1)
            ps = filled(act, "ss_t")
            act.wait_ge(max_ok, TILES + 1)
            act.activation(Ps, ps[:, 0, 0:MEM], ACT.Exp, bias=nmx[:, 0:1], scale=scale, accum_out=asum[:, 0:1]
                           ).then_inc(drained("ss_t"), 1)
            ps = filled(act, "ss_p")
            act.activation(PTs.rearrange("p a b -> p (a b)"), ps[:, 0, 0:MEM], ACT.Copy).then_inc(drained("ss_p"), 1)
            ps = filled(act, "ss_o")
            act.activation(qT[:, :, SEQ:], ps[:, 0, 0:P].rearrange("p (h t) -> p h t", h=HEADS), ACT.Copy
                           ).then_inc(drained("ss_o"), 1)
            act.wait_ge(conv_out, 16 * (1 + HALF))
            for j in range(HALF):
                if j < HALF - 1:
                    act.wait_ge(lnx_ok, j + 1)
                else:
                    emptied(act, "lnm")
                act.activation(lsq[:, j, :], cact[:, j, :], ACT.Square).then_inc(lsq_ok, 1)
            emptied(act, "lnv")
            act.activation(lrs, lrs, ACT.Sqrt).then_inc(lr_ok, 1)
            act.wait_ge(y_in, 16)
            for j in range(HALF):
                act.activation(zz[:, j, 0:SEQ].rearrange("p (c i) -> p i c", i=L),
                               zg[:, j, 0:SEQ].rearrange("p (i c) -> p i c", i=L), ACT.Gelu)
                act.activation(zz[:, j, SEQ:].rearrange("p (b t) -> p t b", b=NB),
                               zg[:, j, SEQ:].rearrange("p (t b) -> p t b", b=NB), ACT.Gelu).then_inc(zz_ok, 1)
            for j in range(HALF):
                act.wait_ge(lnx_ok, HALF + j)
                act.activation(cact[:, j, :], cact[:, j, :], ACT.Silu, bias=c("lb", j)).then_inc(cact_ok, 1)
            act.wait_ge(zz_ok, HALF)
            for j in range(4):
                ps = filled(act, f"glu{j}")
                act.activation(halves(zg[:, j, :]), two(ps), ACT.Sigmoid, bias=c("glu_b", j)
                               ).then_inc(drained(f"glu{j}"), 1)
            act.wait_ge(mem_out, 32)
            with act.Fori(0, 4) as i:
                for r in range(2):
                    for b in range(3):
                        job = GATE0 + 6 * r + b
                        act.wait_ge(full[job % 4], job // 4 + 1 + 3 * i)
                        act.wait_ge(merged_ok, 2 * r + 4 * i)
                        act.activation(halves(gsg[:, r, b, :]), two(pairs[job % 4]), ACT.Sigmoid,
                                       bias=const[:, bass.ds(16 + 8 * b + r + 2 * i, 1)]
                                       ).then_inc(free[job % 4], 1)
            for k in range(KD):
                emptied(act, f"o{k}")
                act.activation(h2sq[:, k, :], h2T[:, k, :], ACT.Square).then_inc(h2sq_ok, 1)
            emptied(act, "ss2")
            act.activation(h2r, h2r, ACT.Sqrt).then_inc(h2r_ok, 1)
            for t in range(TILES + 1):
                ps = filled(act, f"xt{t}")
                act.activation(xb[:, t, :], flat(ps, 1024), ACT.Copy).then_inc(drained(f"xt{t}"), 1)
                ps = filled(act, f"ht{t}")
                rows = P if t < TILES else NB * NT
                act.activation(h2[0:rows, t, :], flat(ps, 1024)[0:rows, :], ACT.Copy).then_inc(drained(f"ht{t}"), 1)
            with act.Fori(0, 4) as i:
                for r in range(2):
                    for b in range(4):
                        job = ROUTE0 + 4 * r + b
                        p = job % 4
                        ps = pairs[p]
                        act.wait_ge(full[p], job // 4 + 1 + 2 * i)
                        if b < 2:
                            act.activation(halves(qbuf[:, b, 0:TOK]), two(ps), ACT.Copy)
                            act.activation(qbuf[:, b, TOK:].rearrange("p (r t) -> p r t", r=3),
                                           ps[:, 1, SEQ - HT:HT].unsqueeze(1).to_broadcast([P, 3, 32]),
                                           ACT.Copy).then_inc(free[p], 1)
                        else:
                            v = sc.rearrange("p (t h) s k -> p t h s k", t=5)
                            act.activation(v[:, :, bass.ds(2 * i + r, 1), b - 2, :].rearrange("p t h k -> p t (h k)"),
                                           flat(ps, 640).rearrange("p (t k) -> p t k", t=5),
                                           ACT.Copy).then_inc(free[p], 1)

            def exp_of(n):
                act.wait_ge(cdiff, n + 1)
                act.activation(ce, cv, ACT.Exp, accum_out=esum).then_inc(cexp, 1)

            def gelu_of(n, par):
                act.wait_ge(u_used, TOPK * n + TOPK)
                act.activation(gel[:, par, :], dots[:, par, :], ACT.Gelu).then_inc(gel_ok, 1)

            def diags(n, lo, hi):
                for j in range(lo, hi):
                    if not (isinstance(n, int) and n == 0 and j < RING):
                        act.wait_ge(v_used, TOPK * n + (j - RING + 1))
                    act.activation(diag[:, j % RING, :], ident, ACT.Copy,
                                   scale=gate.rearrange("p a b -> p (a b)")[:, bass.ds(TOPK * n + j, 1)]
                                   ).then_inc(diag_ok, 1)

            exp_of(0)
            exp_of(1)
            with act.Fori(0, 4) as i:
                for r in range(2):
                    gelu_of(2 * i + r, r)
                    exp_of(2 * i + r + 2)
            for t in range(1, TILES):
                def step(n, r):
                    act.wait_ge(w_ok, n - PH + 1)
                    diags(n - PH, 0, RING)
                    gelu_of(n, r)
                    exp_of(n + 2)
                    diags(n - PH, RING, TOPK)
                if t == 1:
                    step(PH, 0)
                    step(PH + 1, 1)
                with act.Fori(4 * t + (t == 1), 4 * t + 4) as i:
                    step(2 * i, 0)
                    step(2 * i + 1, 1)
                finish_act(act, t - 1, P)
            with act.Fori(12, 15) as i:
                for r in range(2):
                    act.wait_ge(w_ok, 2 * i + r + 1)
                    diags(2 * i + r, 0, RING)
                    exp_of(2 * i + r + 10)
                    diags(2 * i + r, RING, TOPK)
            act.wait_ge(w_ok, TILES * PH)
            diags(30, 0, TOPK)
            diags(31, 0, TOPK)
            finish_act(act, TILES - 1, P)
            n = TOPK * TILES * PH
            act.wait_ge(u_used, n + 32)
            act.activation(gel.rearrange("p a b -> p (a b)"), dots.rearrange("p a b -> p (a b)"), ACT.Gelu
                           ).then_inc(gel_ok, 1)
            act.wait_ge(w_ok, TILES * PH + 1)
            for j in range(32):
                act.wait_ge(v_used, n + j - RING + 1)
                act.activation(diag[:, j % RING, 0:32], fold, ACT.Copy, scale=gate_s[:, j:j + 1]).then_inc(diag_ok, 1)
            finish_act(act, TILES, NB * NT)

        @block.vector
        def _(dve):
            steps = [0]

            def link(ins):
                steps[0] += 1
                ins.then_inc(dve_step, 1)
                dve.wait_ge(dve_step, steps[0])

            tt, ts, stt = dve.tensor_tensor, dve.tensor_scalar, dve.scalar_tensor_tensor
            W = 9 * G

            def tb(i):
                return at(tab + 288 * i, 9, G)

            dt = at(tab + 2336, G)
            one = at(tab + 2368, G)
            two_ = at(tab + 2400, G)
            three = at(tab + 2432, G)
            four = at(tab + 2464, G)
            five = at(tab + 2496, G)
            a_re, a_im = s5p[:, G:2 * G], s5p[:, 2 * G:3 * G]
            link(dve.memset(sgn[0:64, :], -1.0))
            link(dve.memset(sgn[64:P, :], 1.0))
            dve.wait_ge(s5_in, 16)
            dve.wait_ge(s5_scan_in, 1)
            link(ts(one, at(tab, G), -1.0, 1.0, ALU.mult, ALU.add))
            link(dve.reciprocal(two_, one))
            link(ts(one, at(tab, G), 1.0, None, ALU.add))
            link(tt(dt, one, two_, ALU.mult))
            for _ in range(3):
                link(tt(dt, dt, dt, ALU.mult))
            link(tt(one, a_im, dt, ALU.mult))
            link(tt(two_, a_re, dt, ALU.mult))
            for s in range(9):
                link(ts(tb(0)[:, s, :], one, float(8 - s), None, ALU.mult))
                link(ts(tb(2)[:, s, :], two_, float(8 - s), None, ALU.mult))
            th, ki, q1 = at(tab, W), at(tab + 288, W), at(tab + 288 * 5, W)
            link(ts(q1, th, 1.0 / (2 * PI), None, ALU.mult))
            link(dve.tensor_copy(ki.bitcast(I32), q1))
            link(dve.tensor_copy(q1, ki.bitcast(I32)))
            link(stt(th, q1, -TWO_PI_HI, th, ALU.mult, ALU.add))
            link(stt(th, q1, -TWO_PI_LO, th, ALU.mult, ALU.add))
            link(ts(th, th, -PI, PI, ALU.max, ALU.min))
            link(ts(q1, th, -1.0, None, ALU.mult))
            link(tt(q1, q1, th, ALU.max))
            link(ts(at(tab + 288, W), q1, -1.0, PI / 2, ALU.mult, ALU.add))
            link(dve.tensor_copy(at(tab + 2304, G), tb(0)[:, 7, :]))
            dve.sem_inc(epad_ok, 1)
            dve.wait_ge(s5_scan_in, 3)
            t_, m_, sn, cs = tb(2), tb(5), tb(3), tb(4)
            link(ts(m_, t_, -1.0, 1.0, ALU.mult, ALU.add))
            link(dve.reciprocal(tb(6), m_))
            link(ts(m_, t_, 1.0, None, ALU.add))
            link(tt(m_, m_, tb(6), ALU.mult))
            em1 = three
            link(stt(em1, t_[:, 7, :], 2.0, tb(6)[:, 7, :], ALU.mult, ALU.mult))
            link(tt(em1, em1, cs[:, 7, :], ALU.mult))
            half = at(tab + 2304, G)
            link(tt(half, half, half, ALU.mult))
            nr, ni = em1, four
            link(stt(nr, half, -2.0, em1, ALU.mult, ALU.add))
            Lre, Lim = tb(3), tb(4)
            link(tt(tb(0), m_, cs, ALU.mult))
            link(tt(tb(1), m_, sn, ALU.mult))
            Lre, Lim = tb(0), tb(1)
            link(dve.tensor_copy(ni, Lim[:, 7, :]))
            link(tt(one, a_re, a_re, ALU.mult))
            link(tt(two_, a_im, a_im, ALU.mult))
            link(tt(one, one, two_, ALU.add))
            link(dve.reciprocal(two_, one))
            link(tt(one, nr, a_re, ALU.mult))
            link(tt(five, ni, a_im, ALU.mult))
            link(tt(one, one, five, ALU.add))
            link(tt(one, one, two_, ALU.mult))
            link(tt(five, ni, a_re, ALU.mult))
            link(tt(nr, nr, a_im, ALU.mult))
            link(tt(five, five, nr, ALU.subtract))
            link(tt(two_, five, two_, ALU.mult))
            fr = one.unsqueeze(1).to_broadcast([P, 8, G])
            fi = two_.unsqueeze(1).to_broadcast([P, 8, G])
            g1, g2, gt = tb(2)[:, 1:, :], tb(3)[:, 1:, :], tb(4)[:, 1:, :]
            link(tt(g1, Lre[:, 1:, :], fr, ALU.mult))
            link(tt(gt, Lim[:, 1:, :], fi, ALU.mult))
            link(tt(g1, g1, gt, ALU.subtract))
            link(tt(g2, Lim[:, 1:, :], fr, ALU.mult))
            link(tt(gt, Lre[:, 1:, :], fi, ALU.mult))
            link(tt(g2, g2, gt, ALU.add))
            link(ts(g2, g2, sgn[:, 0:1], None, ALU.mult))
            ps = filled(dve, "ssm")
            ts(mr, ps[:, 0, 0:MEM], 1.0 / D, RMS_EPS, ALU.mult, ALU.add).then_inc(free[0], 1)
            dve.wait_ge(consts_in, 16)
            dve.wait_ge(rms_ok, 1)
            link(dve.reciprocal(mr, mr))
            for k in range(KD):
                stt(memT[:, k, :], memT[:, k, :], c("gm", k), mr, ALU.mult, ALU.mult).then_inc(m_ok, 1)
            ps = filled(dve, "ssx")
            ts(halves(xr), two(ps), 1.0 / D, RMS_EPS, ALU.mult, ALU.add).then_inc(free[1], 1)
            dve.wait_ge(rms_ok, 2)
            link(dve.reciprocal(xr, xr))
            for k in range(KD):
                stt(nT[:, k, :], nT[:, k, :], c("g1", k), xr, ALU.mult, ALU.mult).then_inc(n_ok, 1)
            s5B = s5p[:, 3 * G:3 * G + 2 * G * CG].rearrange("p (a g i) -> p a g i", a=2, g=G)
            s5C = s5p[:, 3 * G + 2 * G * CG:].rearrange("p (a g i) -> p a g i", a=2, g=G)
            link(dve.memset(Epad[:, :, L:, :], 0.0))
            tmp = CL.rearrange("p g s i -> p (g s i)").rearrange("p (s x) -> p s x", s=L)

            def bs(v):
                return v.rearrange("p g i -> p (g i)").rearrange("p (g i) -> p g i", i=CG)

            for s in range(L):
                e = Epad[:, :, s, :]
                t1 = tmp[:, s, :].rearrange("p (g i) -> p g i", i=CG)
                tt(t1, s5B[:, 1], g2[:, s, :].unsqueeze(2).to_broadcast([P, G, CG]), ALU.mult)
                link(tt(e, s5B[:, 0], g1[:, s, :].unsqueeze(2).to_broadcast([P, G, CG]), ALU.mult))
                link(tt(e, e, t1, ALU.add))
            h1, h2_ = tb(2)[:, 0:8, :], tb(3)[:, 0:8, :]
            link(ts(h1, Lre[:, 0:8, :], sgn[:, 0:1], -1.0, ALU.mult, ALU.mult))
            link(ts(h2_, Lim[:, 0:8, :], -1.0, None, ALU.mult))
            ct = at(tab + 288 * 4, G, CG)
            for i in range(L):
                s = L - 1 - i
                e = CL[:, :, i, :]
                tt(ct, s5C[:, 1], h2_[:, s, :].unsqueeze(2).to_broadcast([P, G, CG]), ALU.mult)
                link(tt(e, s5C[:, 0], h1[:, s, :].unsqueeze(2).to_broadcast([P, G, CG]), ALU.mult))
                link(tt(e, e, ct, ALU.add))
            link(ts(s5C[:, 0], s5C[:, 0], sgn[:, 0:1], -1.0, ALU.mult, ALU.mult))
            for e in range(2):
                link(dve.tensor_copy(A8[:, e, :], Lre[:, 0, :]))
            link(ts(B8[:, 0, :], Lim[:, 0, :], sgn[:, 0:1], None, ALU.mult))
            link(ts(B8[:, 1, :], B8[:, 0, :], -1.0, None, ALU.mult))
            link(dve.tensor_copy(A4, Lre[:, 4, :]))
            link(ts(B4, Lim[:, 4, :], sgn[:, 0:1], None, ALU.mult))
            dve.sem_inc(epad_ok, 1)
            hist = ain[:, :, ARUN:].rearrange("p c (b k) -> p c b k", b=NB)
            dve.wait_ge(ubuf_ok, 16)
            acol = ain.rearrange("p c n -> p (c n)")
            ccol = cact.rearrange("p c n -> p (c n)")
            with dve.Fori(0, HALF) as j:
                dve.wait_ge(ain_ok, j + 1)
                n = 0
                for k in range(TAPS):
                    w = const[:, bass.ds(COLS["cw"][0] + k + TAPS * j, 1)]
                    for v, src in (
                            (ccol[:, bass.ds(TOK * j, SEQ)], acol[:, bass.ds(AIN * j + k, SEQ)]),
                            (ccol[:, bass.ds(TOK * j + SEQ, NB * NT)].rearrange("p (b t) -> p b t", b=NB),
                             acol[:, bass.ds(AIN * j + ARUN, NB * SRUN)]
                             .rearrange("p (b t) -> p b t", b=NB)[:, :, k:k + NT])):
                        if k == 0:
                            ts(v, src, w, const[:, bass.ds(COLS["cb"][0] + j, 1)], ALU.mult, ALU.add
                               ).then_inc(conv_step, 1)
                        else:
                            dve.wait_ge(conv_step, n - 1 + 2 * TAPS * j)
                            stt(v, src, w, v, ALU.mult, ALU.add).then_inc(conv_step, 1)
                        n += 1
            for e in range(2):
                for h in range(2):
                    emptied(dve, f"z{e}{h}")
            link(dve.memset(Z[:, :, :, 0:1], 0.0))
            flatZ = Z.rearrange("p e g c -> p (e g) c")
            per = 4 * 3
            with dve.Fori(0, NC // 4) as i:
                for r in range(4):
                    n = 3 * r
                    src = flatZ[:, :, bass.ds(4 * i + r, 1)].rearrange("p a b -> p (a b)")
                    dst = flatZ[:, :, bass.ds(4 * i + r + 1, 1)].rearrange("p a b -> p (a b)")
                    tt(dve_t[:, 0, :], src, A8.rearrange("p a b -> p (a b)"), ALU.mult)
                    for e in range(2):
                        ins = tt(dve_t[:, 1, e * G:(e + 1) * G],
                                 flatZ[:, (1 - e) * G:(2 - e) * G, bass.ds(4 * i + r, 1)]
                                 .rearrange("p a b -> p (a b)"), B8[:, e, :], ALU.mult)
                    ins.then_inc(scan_step, 1)
                    dve.wait_ge(scan_step, n + 1 + per * i)
                    tt(dve_t[:, 0, :], dve_t[:, 0, :], dve_t[:, 1, :], ALU.add).then_inc(scan_step, 1)
                    dve.wait_ge(scan_step, n + 2 + per * i)
                    tt(dst, dst, dve_t[:, 0, :], ALU.add).then_inc(scan_step, 1)
                    dve.wait_ge(scan_step, n + 3 + per * i)
            dve.tensor_copy(dve_t[:, 0, 0:G], Z[:, 0, :, NC]).then_inc(scan_ok, 1)
            scale = float(P) ** -0.5
            for t in range(TILES):
                ps = flat(filled(dve, f"as{t}"), 1024).rearrange("p (h m) -> p h m", h=HEADS)
                link(dve.tensor_reduce(mx, ps, AX.X, ALU.max))
                ts(nmx, mx, -scale, None, ALU.mult).then_inc(max_ok, 1)
                emptied(dve, f"as{t}")
                link(dve.reciprocal(ars, asum))
                tt(Pm, Pm, ars.unsqueeze(2).to_broadcast([P, HEADS, MEM]), ALU.mult).then_inc(p_ok, 1)
            ps = filled(dve, "ss_t")
            link(dve.tensor_reduce(mx[:, 0:1], ps[:, 0, 0:MEM], AX.X, ALU.max))
            ts(nmx[:, 0:1], mx[:, 0:1], -scale, None, ALU.mult).then_inc(max_ok, 1)
            emptied(dve, "ss_t")
            link(dve.reciprocal(ars[:, 0:1], asum[:, 0:1]))
            ts(Ps, Ps, ars[:, 0:1], None, ALU.mult).then_inc(p_ok, 1)
            for h in range(2):
                ps = flat(filled(dve, f"y{h}"), 1024).rearrange("p (g n) -> p g n", g=16)
                for g in range(16):
                    ins = stt(Y[:, 16 * h + g, :], U[:, 16 * h + g, :], c("d", 16 * h + g), ps[:, g, :],
                              ALU.mult, ALU.add)
                ins.then_inc(drained(f"y{h}"), 1)
            ps = filled(dve, "ys")
            for g in range(G):
                ins = stt(Ys[:, g, :], Us[:, g, :], c("d", g), ps[:, 0, NB * g:NB * (g + 1)], ALU.mult, ALU.add)
            ins.then_inc(drained("ys"), 1)
            dve.wait_ge(h0_in, 16)
            ps = filled(dve, "zs")
            hv = h0
            link(tt(hv[:, 1], hv[:, 1], B4.unsqueeze(2).to_broadcast([P, G, NB]), ALU.mult))
            link(tt(hv[:, 0], hv[:, 0], A4.unsqueeze(2).to_broadcast([P, G, NB]), ALU.mult))
            link(tt(hv[:, 0], hv[:, 0], hv[:, 1], ALU.add))
            tt(hv[:, 0], hv[:, 0], ps[:, 0, 0:G * NB].rearrange("p (g b) -> p g b", g=G), ALU.add
               ).then_inc(drained("zs"), 1)
            ps = filled(dve, "lnm")
            for j in range(HALF):
                ins = stt(halves(cact[:, j, :]), two(ps), -1.0 / 512, halves(cact[:, j, :]), ALU.mult, ALU.add)
                if j < HALF - 1:
                    ins.then_inc(lnx_ok, 1)
            ins.then_inc(drained("lnm"), 1)
            ps = filled(dve, "lnv")
            ts(halves(lrs), two(ps), 1.0 / 512, LN_EPS, ALU.mult, ALU.add).then_inc(drained("lnv"), 1)
            dve.wait_ge(lr_ok, 1)
            link(dve.reciprocal(lrs, lrs))
            for j in range(HALF):
                stt(cact[:, j, :], cact[:, j, :], c("lg", j), lrs, ALU.mult, ALU.mult).then_inc(lnx_ok, 1)
            for j in range(HALF):
                p, n = JOB[f"glu{j}"]
                dve.wait_ge(free[p], n + 1)
                tt(zg[:, j, :], zg[:, j, :], zz[:, j, :], ALU.mult).then_inc(zg_ok, 1)
            mflat = merged.rearrange("p k t -> p (k t)")
            with dve.Fori(0, 4) as i:
                for r in range(2):
                    dst = mflat[:, bass.ds((2 * i + r) * TOK, TOK)]
                    for b in range(3):
                        gj, job = GATE0 + 6 * r + b, GATE0 + 6 * r + 3 + b
                        dve.wait_ge(free[gj % 4], gj // 4 + 1 + 3 * i)
                        dve.wait_ge(full[job % 4], job // 4 + 1 + 3 * i)
                        tt(halves(gtmp if b else dst), halves(gsg[:, r, b, :]), two(pairs[job % 4]), ALU.mult
                           ).then_inc(free[job % 4], 1)
                        dve.wait_ge(free[job % 4], job // 4 + 1 + 3 * i)
                        if b:
                            tt(dst, dst, gtmp, ALU.add).then_inc(merged_ok, 1)
                            dve.wait_ge(merged_ok, 2 * r + b + 4 * i)
            dve.wait_ge(x2_in, 16)
            for j in range(8):
                ps = filled(dve, f"o{j}")
                tt(halves(h2T[:, j, :]), two(ps), halves(h2T[:, j, :]), ALU.add).then_inc(drained(f"o{j}"), 1)
            ps = filled(dve, "ss2")
            ts(halves(h2r), two(ps), 1.0 / D, RMS_EPS, ALU.mult, ALU.add).then_inc(drained("ss2"), 1)
            dve.wait_ge(h2r_ok, 1)
            link(dve.reciprocal(h2r, h2r))
            for k in range(KD):
                link(stt(xbT[:, k, 0:TOK], h2T[:, k, :], c("g2", k), h2r, ALU.mult, ALU.mult))
                dve.tensor_copy(xbT[:, k, TOK:].rearrange("p (r t) -> p r t", r=3),
                                xbT[:, k, SEQ:TOK].unsqueeze(1).to_broadcast([P, 3, 32])).then_inc(xbT_ok, 1)
            dve.wait_ge(iota_ok, 1)
            dve.wait_ge(state_out, 32)
            link(dve.tensor_copy(iota16, iota16.bitcast(I32)))
            link(tt(fold, ident[:, 0:32], ident[:, 32:64], ALU.add))
            link(tt(fold, fold, ident[:, 64:96], ALU.add))
            link(tt(fold, fold, ident[:, 96:128], ALU.add))

            scf = sc.rearrange("p n s k -> p (n s k)")
            expf, gatf = expert.rearrange("p n k -> p (n k)"), gate.rearrange("p n k -> p (n k)")

            def route(n, par, head=None, stage=True):
                local = [0]

                def step(ins):
                    local[0] += 1
                    ins.then_inc(route_step, 1)
                    dve.wait_ge(route_step, local[0])

                if head is not None:
                    for b in (2, 3):
                        job = ROUTE0 + 4 * head + b
                        dve.wait_ge(free[job % 4], job // 4 + 1)
                dve.sem_clear(route_step)
                step(dve.tensor_copy(sw.rearrange("p s k -> p (s k)"), scf[:, bass.ds(n * 2 * P, 2 * P)]))
                for s in range(2):
                    v = sw[:, s, :]
                    step(dve.max(tv[:, s, 0:8], v))
                    step(dve.max_index(tiu[:, s, 0:8], tv[:, s, 0:8], v))
                    step(dve.match_replace(v, tv[:, s, 0:8], v, NEG))
                    step(dve.max(tv[:, s, 8:16], v))
                    step(dve.max_index(tiu[:, s, 8:16], tv[:, s, 8:16], v))
                step(tt(cand, tv[:, 0, :].unsqueeze(2).to_broadcast([P, 16, 16]),
                        tv[:, 1, :].unsqueeze(1).to_broadcast([P, 16, 16]), ALU.add))
                cf = cand.rearrange("p a b -> p (a b)")
                step(dve.max(cv[:, 0:8], cf))
                step(dve.max_index(ciu[:, 0:8], cv[:, 0:8], cf))
                step(dve.match_replace(cf, cv[:, 0:8], cf, NEG))
                step(dve.max(cv[:, 8:16], cf))
                step(dve.max_index(ciu[:, 8:16], cv[:, 8:16], cf))
                step(ts(hlu[:, 0, :], ciu, 4, None, ALU.logical_shift_right))
                step(ts(hlu[:, 1, :], ciu, 15, None, ALU.bitwise_and))
                step(dve.tensor_copy(hlf, hlu))
                step(dve.tensor_copy(tif, tiu))
                step(dve.tensor_copy(i12[:, 0, 0:1], cv[:, 0:1]))
                ts(cv, cv, i12[:, 0, 0:1], None, ALU.subtract).then_inc(cdiff, 1)
                dve.wait_ge(cdiff, n + 1)
                for s in range(2):
                    step(tt(eq, hlf[:, s, :].unsqueeze(2).to_broadcast([P, 16, 16]),
                            iota16.unsqueeze(1).to_broadcast([P, 16, 16]), ALU.is_equal))
                    step(tt(eq, eq, tif[:, s, :].unsqueeze(1).to_broadcast([P, 16, 16]), ALU.mult))
                    step(dve.tensor_reduce(i12[:, s, :], eq, AX.X, ALU.add))
                step(stt(i12[:, 0, :], i12[:, 0, :], 128.0, i12[:, 1, :], ALU.mult, ALU.add))
                step(dve.tensor_copy(expf[:, bass.ds(n * TOPK, TOPK)], i12[:, 0, :]))
                dve.wait_ge(cexp, n + 1)
                step(dve.reciprocal(ers, esum))
                step(ts(gatf[:, bass.ds(n * TOPK, TOPK)], ce, ers, None, ALU.mult))
                if stage:
                    dve.tensor_copy(idx_u[:, par, :], i12[:, 0, :]).then_inc(routed, 1)
                    dve.wait_ge(routed, n + 1)

            def dot(n, par, x):
                for j in range(TOPK):
                    dve.wait_ge(u_in[j % RING], 32 * n + 16 * (j // RING + 1))
                    u = uring[:, j % RING, :]
                    dve.tensor_tensor_reduce(u, u, x, 1.0, 0.0, ALU.mult, ALU.add, dots[:, par, j:j + 1]
                                             ).then_inc(u_used, 1)

            def weigh(n, par):
                dve.wait_ge(gel_ok, n + 1)
                w = gatf[:, bass.ds(n * TOPK, TOPK)]
                tt(w, w, gel[:, par, :], ALU.mult).then_inc(w_ok, 1)

            def stage_v(n, par):
                dve.tensor_copy(idx_v[:, par, :], expf[:, bass.ds(n * TOPK, TOPK)]).then_inc(idxv_ok, 1)

            def add_v(n, par):
                dve.wait_ge(acc_step, n + 1)
                dve.wait_ge(v_used, TOPK * n + TOPK)
                tt(acc, acc, flat(pairs[par], 1024), ALU.add).then_inc(acc_step, 1)

            def finish(t, rows):
                dve.wait_ge(acc_step, min(PH * (t + 1), PH * TILES + 1) + 1)
                dve.sem_inc(acc_ok, 1)
                dve.wait_ge(fsq_ok, t + 1)
                ts(frs[0:rows, :], fss[0:rows, :], 1.0 / D, RMS_EPS, ALU.mult, ALU.add).then_inc(fms_ok, 1)
                dve.wait_ge(frt_ok, t + 1)
                link(dve.reciprocal(frs[0:rows, :], frs[0:rows, :]))
                stt(ytile[0:rows, :], acc[0:rows, :], frs[0:rows, 0:1], gf[0:rows, :], ALU.mult, ALU.mult
                    ).then_inc(yt_ok, 1)

            for t in range(TILES + 1):
                emptied(dve, f"ht{t}")
            route(0, 0, 0)
            route(1, 1, 1)
            for i in range(3):
                for r in range(2):
                    dot(2 * i + r, r, xb[:, 0, :])
                    route(2 * i + r + 2, r, 2 * i + r + 2)
                    weigh(2 * i + r, r)
            for r in range(2):
                dot(6 + r, r, xb[:, 0, :])
                route(8 + r, r)
                weigh(6 + r, r)
            dve.wait_ge(gf_in, 16)
            dve.wait_ge(w_ok, PH)
            stage_v(0, 0)
            stage_v(1, 1)
            for t in range(1, TILES):
                if t > 1:
                    dve.wait_ge(yt_ok, t - 1)
                ins = dve.tensor_copy(acc, h2[:, t - 1, :])
                if t == 1:
                    ins.then_inc(acc_step, 1)
                dve.tensor_copy(xbcur, xb[:, t, :]).then_inc(xload, 1)
                dve.wait_ge(xload, t)

                with dve.Fori(4 * t, 4 * t + 4) as i:
                    for r in range(2):
                        n = 2 * i + r
                        dot(n, r, xbcur)
                        route(n + 2, r)
                        weigh(n, r)
                        add_v(n - PH, r)
                        stage_v(n - PH + 2, r)
                finish(t - 1, P)
            dve.wait_ge(yt_ok, TILES - 1)
            dve.tensor_copy(acc, h2[:, TILES - 1, :]).then_inc(xload, 1)
            dve.wait_ge(xload, TILES)
            with dve.Fori(12, 15) as i:
                for r in range(2):
                    n = 2 * i + r
                    route(n + 10, r, stage=False)
                    add_v(n, r)
                    stage_v(n + 2, r)
            ef = expf[:, TILES * PH * TOPK:].rearrange("p (j q) -> p j q", q=4)
            gq = gatf[:, TILES * PH * TOPK:].rearrange("p (j q) -> p j q", q=4)
            for q in range(4):
                rows = slice(32 * q, 32 * q + 32)
                dve.tensor_copy(idx_s[rows, :], ef[rows, :, q])
                ins = dve.tensor_copy(gate_s[rows, :], gq[rows, :, q])
            ins.then_inc(routed, 1)
            dve.wait_ge(routed, TILES * PH + 3)
            add_v(30, 0)
            add_v(31, 1)
            finish(TILES - 1, P)
            for j in range(32):
                dve.wait_ge(u_in[j % RING], 16 * (2 * TILES * PH + j // RING + 1))
                u = uring[:, j % RING, :]
                dve.tensor_tensor_reduce(u, u, xb[:, TILES, :], 1.0, 0.0, ALU.mult, ALU.add,
                                         dots.rearrange("p a b -> p (a b)")[:, j:j + 1]).then_inc(u_used, 1)
            dve.wait_ge(gel_ok, TILES * PH + 1)
            tt(gate_s, gate_s, gel.rearrange("p a b -> p (a b)"), ALU.mult).then_inc(w_ok, 1)
            dve.wait_ge(v_used, TOPK * TILES * PH + 32)
            dve.wait_ge(yt_ok, TILES)
            tt(acc[0:32, :], h2[0:32, TILES, :], flat(pairs[0], 1024)[0:32, :], ALU.add).then_inc(acc_step, 1)
            finish(TILES, NB * NT)


OUTS = (("y", (TOK, D)), ("ssm_p", (P, G)), ("ssm_s", (P, G, NB)), ("conv_p", (P, HALF, PAD)),
        ("conv_s", (P, HALF, NB, PAD)), ("mem_k", (P, HEADS, MEM)), ("mem_v", (P, 2, 512)))


def kernel(x_prompt, x_sample, mem_prompt, state_ssm_re, state_ssm_im, state_conv,
           cache_mem_k, cache_mem_v, norm1_g, w_in, b_in, s5_log_dt, s5_a_re, s5_a_im,
           s5_b_re, s5_b_im, s5_c_re, s5_c_im, s5_d, s5_glu_w, s5_glu_b, w_s5_proj,
           conv_dw_w, conv_dw_b, conv_ln_g, conv_ln_b, w_conv_proj, mem_norm_g,
           w_mem_k, w_mem_v, w_xa_proj, w_out, norm2_g, peer_w_q, peer_sub_keys,
           peer_u, peer_v, final_norm_g):
    import numpy as np
    import concourse.bacc as bacc
    from concourse.bass_utils import run_bass_kernel_spmd

    def cols(v):
        return np.asarray(v).reshape(-1, P).T

    def blocks(w):
        w = np.asarray(w)
        k, m = w.shape
        return np.ascontiguousarray(w.reshape(k // P, P, m // P, P).transpose(2, 1, 0, 3)).reshape(m // P, P, k)

    def stack(re, im):
        re, im = np.asarray(re), np.asarray(im)
        return np.concatenate([np.moveaxis(re, 1, 0), np.moveaxis(im, 1, 0)], 0)

    x = np.concatenate([np.asarray(x_prompt)[0], np.asarray(x_sample).reshape(NB * NT, D)], 0)
    conv_w = np.asarray(conv_dw_w)[0].T.reshape(HALF, P, TAPS).transpose(1, 0, 2).reshape(P, HALF * TAPS)
    keys = np.asarray(peer_sub_keys)[0].transpose(2, 0, 1).reshape(P, 2 * P)
    d_rows = np.tile(np.asarray(s5_d)[0].T, (L, 1))
    consts = np.concatenate([cols(b_in[0]), cols(norm1_g[0]), cols(mem_norm_g[0]), cols(norm2_g[0]),
                             cols(s5_glu_b[0]), conv_w, cols(conv_dw_b[0]), cols(conv_ln_g[0]),
                             cols(conv_ln_b[0]), d_rows, keys], 1)
    br, bi, cr, ci = (np.asarray(v)[0] for v in (s5_b_re, s5_b_im, s5_c_re, s5_c_im))
    cr, ci = cr.transpose(0, 2, 1), ci.transpose(0, 2, 1)
    ar, ai = np.asarray(s5_a_re)[0], np.asarray(s5_a_im)[0]
    s5 = np.concatenate([np.tile(np.asarray(s5_log_dt), (P, 1)), stack(ar, ar), stack(ai, ai)]
                        + [stack(*v).reshape(P, G * CG) for v in ((br, bi), (bi, br), (cr, ci), (ci, cr))], 1)
    hr, hi = (np.asarray(v)[0].transpose(1, 2, 0) for v in (state_ssm_re, state_ssm_im))
    given = {
        "x_t": x.T.reshape(KD, P, TOK).transpose(1, 0, 2),
        "mem_t": np.asarray(mem_prompt)[0].T.reshape(KD, P, MEM).transpose(1, 0, 2),
        "consts": consts, "s5_pack": s5,
        "h0": np.stack([stack(hr, hi), stack(hi, hr)], 1).reshape(P, 2 * G * NB),
        "conv_hist": np.asarray(state_conv)[0].transpose(2, 0, 1).reshape(HALF, P, NB, PAD).transpose(1, 0, 2, 3),
        "cache_k": np.asarray(cache_mem_k)[0].transpose(0, 3, 2, 1).reshape(NB, P, HEADS * MEM),
        "cache_v": np.asarray(cache_mem_v)[0].reshape(NB, 2, P, 512).transpose(0, 2, 1, 3).reshape(NB, P, 1024),
        "w_in": blocks(w_in[0]), "w_mem_k": blocks(w_mem_k[0]), "w_mem_v": blocks(w_mem_v[0]),
        "glu_w": blocks(s5_glu_w[0]),
        "proj": np.stack([blocks(w[0]) for w in (w_s5_proj, w_conv_proj, w_xa_proj)]),
        "w_out": blocks(w_out[0]), "peer_q": blocks(peer_w_q[0]),
        "peer_u": np.asarray(peer_u)[0], "peer_v": np.asarray(peer_v)[0],
        "final_g": np.asarray(final_norm_g),
    }
    nc = bacc.Bacc("TRN2", target_bir_lowering=False, num_devices=1)
    given = {f"in_{k}": np.ascontiguousarray(v) for k, v in given.items()}
    a = {k[3:]: nc.dram_tensor(k, v.shape, mybir.dt.from_np(v.dtype), kind="ExternalInput").ap()
         for k, v in given.items()}
    o = {k: nc.dram_tensor(f"out_{k}", shape, F32, kind="ExternalOutput").ap() for k, shape in OUTS}
    hybrid_step(nc, a, o)
    got = run_bass_kernel_spmd(nc, [given], core_ids=[0]).results[0]
    y, sp, ss, cp, cs, mk, mv = (np.asarray(got[f"out_{k}"]) for k, _ in OUTS)

    def rows(v):
        return v[0:N], v[N:P]

    pr, pi = (v.T.reshape(1, 1, G, N) for v in rows(sp))
    sr, si = (v.transpose(2, 1, 0).reshape(1, NB, G, N) for v in rows(ss))
    return (y[0:SEQ].reshape(1, SEQ, D), y[SEQ:].reshape(NB, NT, D), pr, pi,
            cp.transpose(2, 1, 0).reshape(1, 1, PAD, 512),
            mk.transpose(2, 1, 0).reshape(1, 1, MEM, HEADS, P),
            mv.transpose(1, 0, 2).reshape(1, 1, MEM, HEADS, P),
            sr, si, cs.transpose(2, 3, 1, 0).reshape(1, NB, PAD, 512))
```

```python
from contextlib import ExitStack

import concourse.bass as bass
from concourse import mybir

F32 = mybir.dt.float32
F32R = mybir.dt.float32r
I32 = mybir.dt.int32
U32 = mybir.dt.uint32
ALU = mybir.AluOpType
ACT = mybir.ActivationFunctionType
AX = mybir.AxisListType

P = 128
D = 1024
KD = D // P
HALF = 512 // P
SEQ, NB, NT = 512, 8, 4
TOK = SEQ + NB * NT
HT = TOK // 2
G, N, CG = 32, 64, 16
L = 8
NC = SEQ // L
TAPS = 31
PAD = TAPS - 1
ARUN = PAD + SEQ
SRUN = PAD + NT
AIN = ARUN + NB * SRUN
HEADS = 4
MEM = 256
PH = 8
TOPK = 16
TILES = SEQ // P
RMS_EPS, LN_EPS = 1e-6, 1e-5
PI = 3.141592653589793
TWO_PI_HI = 6.28125
TWO_PI_LO = 2 * PI - TWO_PI_HI
NEG = -3.0e38
RING = 8
LAG = 2

COLS, _at = {}, 0
for _name, _n in (("b_in", 40), ("g1", 8), ("gm", 8), ("g2", 8), ("glu_b", 4), ("cw", 4 * TAPS),
                  ("cb", 4), ("lg", 4), ("lb", 4), ("d", G), ("keys", 256)):
    COLS[_name] = (_at, _n)
    _at += _n
N_CONST = _at
N_S5 = 3 * G + 4 * G * CG

JOBS = (["ssm", "ssx"] + [f"k{c}" for c in range(4)] + ["v"]
        + [f"{a}{c}" for c in range(4) for a in ("ag", "ai")]
        + [f"u{c}" for c in range(4)]
        + ["T"] + [f"ET{b}" for b in range(4)]
        + ["q0", "q1"]
        + [f"z{e}{h}" for e in range(2) for h in range(2)]
        + ["q2", "q3"]
        + ["ss_s", "ys", "zs", "lnm", "y0", "y1"]
        + ["as0", "as1", "lnv", "at0", "ao0", "as2", "at1", "ao1", "as3", "at2", "ao2", "at3", "ao3"]
        + ["ss_t", "ss_p", "ss_o"]
        + [f"glu{c}" for c in range(4)])
LOOP_JOBS = 12
JOB_NUMBER = {n: i for i, n in enumerate(JOBS)}
GATE0 = len(JOBS)
_after = _after_jobs = GATE0 + 4 * LOOP_JOBS
TAIL = [f"o{c}" for c in range(8)] + ["ss2"] + [f"ht{t}" for t in range(5)]
for _i, _n in enumerate(TAIL):
    JOB_NUMBER[_n] = _after + _i
JOB = {n: (i % 4, i // 4) for n, i in JOB_NUMBER.items()}
ROUTE0 = _after + len(TAIL)
BEFORE_ROUTE = [(ROUTE0 - p + 3) // 4 for p in range(4)]
for _t in range(TILES + 1):
    JOB[f"xt{_t}"] = (_t % 2, BEFORE_ROUTE[_t % 2] + _t // 2)

LOADS = ([f"k{c}" for c in range(4)] + [f"v{c}" for c in range(4)]
         + [f"{a}{c}" for c in range(4) for a in ("ag", "ai")]
         + [f"u{c}" for c in range(4)] + [f"q{c}" for c in range(4)] + [f"glu{c}" for c in range(4)])
WS = 6
LOAD = {n: (i % WS, i // WS) for i, n in enumerate(LOADS)}
WGATE0 = len(LOADS)
_after = WGATE0 + 48
for _c in range(8):
    LOAD[f"o{_c}"] = ((_after + _c) % WS, (_after + _c) // WS)
WROUTE0 = _after + 8
LOADED_BEFORE = {n: JOB_NUMBER["v" if LOADS[i - WS][0] == "v" else LOADS[i - WS]]
                 for i, n in enumerate(LOADS) if i >= WS}
for _c in range(8):
    LOADED_BEFORE[f"o{_c}"] = _after_jobs - 6 + _c if _c < 6 else JOB_NUMBER[f"o{_c - 6}"]


def hybrid_step(nc, a, o):
    ctx = ExitStack()
    with ctx:
        def sem(name):
            return ctx.enter_context(nc.semaphore(name))

        R = 10496
        ROUNDED = {
            "whigh": (0, WS, 1024),
            "nTl": (R + 18688, KD, TOK),
            "wl": (R + 23040, 4608),
            "zl": (R, HALF, TOK),
            "ql": (R + 35992, HALF, TOK),
            "cl": (R + 38168, HALF, TOK),
            "ml": (R + 14336, KD, TOK),
            "nTh": (6144, KD, TOK),
            "mh": (R + 4096, KD, TOK),
            "zh": (R + 10240, HALF, TOK),
            "ch": (R + 27832, HALF, TOK),
            "qh": (R + 30008, HALF, TOK),
        }
        over = {}
        for name, (start, *shape) in ROUNDED.items():
            n = shape[0] * (shape[1] if len(shape) > 1 else 1)
            with ExitStack() as place:
                if start:
                    place.enter_context(nc.sbuf_tensor(f"before_{name}", [P, start], F32))
                over[name] = place.enter_context(nc.sbuf_tensor(name, [P, n], F32R))[:, :]
        SPLIT_AT, WORDS = 24832, 52992
        arenas = [ctx.enter_context(nc.sbuf_tensor(name, [P, size], F32))
                  for name, size in (("lower", SPLIT_AT), ("upper", WORDS - SPLIT_AT))]
        pairs = [ctx.enter_context(nc.psum_tensor(f"pair{i}", [P, 2, 512], F32)) for i in range(4)]
        ubuf = nc.dram_tensor("ubuf", [G * CG, TOK], F32, kind="Internal").ap()
        ybuf = nc.dram_tensor("ybuf", [G * CG, TOK], F32, kind="Internal").ap()

        def at(start, *shape):
            n = 1
            for x in shape:
                n *= x
            piece, first = (arenas[0], 0) if start < SPLIT_AT else (arenas[1], SPLIT_AT)
            v = piece[:, start - first:start - first + n]
            names = "abcd"[:len(shape)]
            if len(shape) > 1:
                v = v.rearrange(f"p ({' '.join(names)}) -> p {' '.join(names)}",
                                **{x: s for x, s in zip(names[1:], shape[1:])})
            return v

        def rounded(name):
            shape = ROUNDED[name][1:]
            v = over[name]
            return v if len(shape) == 1 else v.rearrange("p (a b) -> p a b", a=shape[0])

        wring = at(0, WS, 1024)
        nT = at(6144, KD, TOK)
        Tm = at(R, L, CG, G)
        zz = at(R, HALF, TOK)
        ET = at(R + 4096, G, 192)
        xsq = at(R + 4096, KD, TOK)
        merged = at(R + 4096, KD, TOK)
        CL = at(R + 10240, G, L, CG)
        zg = at(R + 10240, HALF, TOK)
        Epad = at(R + 14336, G, 15, CG)
        Z = at(R + 14336, 2, G, NC + 1)
        Y = at(R + 14336 + 4160, G, NC)
        Ys = at(R + 14336 + 4160 + 2048, G, NB)
        h2T = at(R + 18688, KD, TOK)
        U = at(R + 22016, G, NC)
        Us = at(R + 24064, G, NB)
        Us2 = at(R + 24320, G, NB)
        tab = R + 22016
        ain = at(R + 24576, HALF, AIN)
        memT = at(R + 24576, KD, MEM)
        cact = at(R + 27832, HALF, TOK)
        msq = at(R + 27832, KD, MEM)
        qT = at(R + 30008, HALF, TOK)
        kT = at(R + 32184, HEADS, MEM)
        vm = at(R + 33208, 2, 512)
        Pm = at(R + 34232, HEADS, MEM)
        PT = at(R + 35256, HEADS, 2, P)
        sg = at(R + 34232, 2, TOK)
        xr = at(R + 35328, TOK)
        mr = at(R + 35328 + TOK, MEM)
        ctmp = at(R + 35328, 3, HALF, NB, NT)
        ut = at(R + 8064, HALF, TOK)
        gsg = at(R + 32184, 2, 3, TOK)
        gtmp = at(R + 32184 + 6 * TOK, TOK)
        lsq = at(R + 24576, HALF, TOK)
        lrs = at(R + 24576 + HALF * TOK, TOK)
        cring = at(R + 36280, 3, 1024)
        s5p = at(R + 36280, N_S5)
        h0 = at(R + 39352, 2, G, NB)
        ST = at(R + 39864, 2, P)
        Ps = at(R + 40120, MEM)
        PTs = at(R + 40376, 2, P)
        C0 = R + 40632
        const = at(C0, N_CONST)
        ident = at(C0 + N_CONST, P)
        ones = at(C0 + N_CONST + P, P)
        SM = C0 + N_CONST + 2 * P
        mx, nmx, asum, ars = (at(SM + 4 * i, 4) for i in range(4))
        sgn = at(SM + 16, 1)
        A8 = at(SM + 20, 2, G)
        B8 = at(SM + 84, 2, G)
        A4 = at(SM + 148, G)
        B4 = at(SM + 180, G)
        dve_t = at(SM + 212, 2, 64)
        xbT = at(6144, KD, 5 * P)
        h2 = at(11264, 5, D)
        sw = at(16384, 2, P)
        uring = at(16640, RING, D)
        vring = at(24832, RING, D)
        h2sq = at(6144, KD, TOK)
        h2r = at(33536, TOK)
        diag = at(33024, RING, P)
        sc = at(34080, 5 * PH, 2, P)
        xb = at(44320, 5, D)
        expert = at(49440, 5 * PH, TOPK).bitcast(U32)
        gate = at(50080, 5 * PH, TOPK)
        Q0 = 50720
        dots = at(Q0, 2, TOPK)
        gel = at(Q0 + 32, 2, TOPK)
        idx_u = at(Q0 + 64, 2, TOPK).bitcast(U32)
        idx_v = at(Q0 + 96, 2, TOPK).bitcast(U32)
        idx_s = at(Q0 + 128, 32).bitcast(U32)
        gate_s = at(Q0 + 160, 32)
        fold = at(Q0 + 192, 32)
        esum, ers = at(Q0 + 224, 1), at(Q0 + 225, 1)
        fss, frs = at(Q0 + 226, 1), at(Q0 + 227, 1)
        iota16 = at(Q0 + 228, TOPK)
        qbuf = at(4096, 2, 5 * P)
        cand = at(5376, 16, 16)
        eq = at(5632, 16, 16)
        tv = at(5888, 2, TOPK)
        tif = at(5920, 2, TOPK)
        tiu = at(5952, 2, TOPK).bitcast(U32)
        cv = at(5984, TOPK)
        ciu = at(6000, TOPK).bitcast(U32)
        hlu = at(6016, 2, TOPK).bitcast(U32)
        hlf = at(6048, 2, TOPK)
        i12 = at(6080, 2, TOPK)
        ce = at(6112, TOPK)
        ytile = at(8192, D)
        gf = at(9216, D)

        def c(name, i=0, n=1):
            s = COLS[name][0] + i
            return const[:, s:s + n]

        whigh, nTl, wl, zl, ql, cl, ml, nTh, mh, zh, ch, qh = (rounded(name) for name in ROUNDED)

        consts_in, s5_in, x_in, mem_in, h0_in = (sem(n) for n in ("consts_in", "s5_in", "x_in", "mem_in", "h0_in"))
        w_in = [sem(f"w_in{i}") for i in range(WS)]
        full = [sem(f"full{i}") for i in range(4)]
        free = [sem(f"free{i}") for i in range(4)]
        made = sem("made")
        pool_step, dve_step, conv_step, scan_step, route_step = (sem(n) for n in (
            "pool_step", "dve_step", "conv_step", "scan_step", "route_step"))
        msq_ok, xsq_ok, rms_ok, m_ok, n_ok = (sem(n) for n in ("msq_ok", "xsq_ok", "rms_ok", "m_ok", "n_ok"))
        epad_ok, s5_scan_in = sem("epad_ok"), sem("s5_functions_ok")
        split_step, nl_ok, bl_ok, wl_ok, ml_ok = (sem(n) for n in (
            "split_step", "nT_low_ok", "branch_low_ok", "weight_low_ok", "merged_low_ok"))
        ain_zero, ain_ok, conv_out, mem_out, state_out = (sem(n) for n in (
            "ain_history_in", "ain_ok", "conv_out", "mem_out", "state_out"))
        t_zero, t_in = sem("t_zero"), sem("t_in")
        us_zero, ubuf_ok, u_ok, scan_ok, ybuf_ok, y_in = (sem(n) for n in (
            "us_zero", "ubuf_ok", "u_in_chunks", "scan_ok", "ybuf_ok", "y_in"))
        max_ok, p_ok = sem("max_ok"), sem("p_ok")
        cin = [sem(f"cache_in{i}") for i in range(3)]
        c_used = [sem(f"cache_used{i}") for i in range(3)]
        zz_ok, zg_ok, lnx_ok, lsq_ok, lr_ok, cact_ok = (sem(n) for n in (
            "zz_ok", "zg_ok", "lnx_ok", "lsq_ok", "lr_ok", "cact_ok"))
        merged_ok, x2_in, h2sq_ok, h2r_ok, xbT_ok, gf_in, iota_ok = (sem(n) for n in (
            "merged_ok", "x2_in", "h2sq_ok", "h2r_ok", "xbT_ok", "gf_in", "iota_ok"))
        routed, samples_routed, cdiff, cexp = (sem(n) for n in ("routed", "samples_routed", "cdiff", "cexp"))
        u_in = [sem(f"u_in{i}") for i in range(RING)]
        v_in = [sem(f"v_in{i}") for i in range(RING)]
        u_used, v_used, gel_ok, w_ok, idxv_ok, diag_ok = (sem(n) for n in (
            "u_used", "v_used", "gel_ok", "w_ok", "idxv_ok", "diag_ok"))
        slot_free = sem("slot_free")
        acc_step, acc_ok, fsq_ok, fms_ok, frt_ok, yt_ok, yt_out = (sem(n) for n in (
            "acc_step", "acc_ok", "fsq_ok", "fms_ok", "frt_ok", "yt_ok", "yt_out"))

        block = ctx.enter_context(nc.Block())

        def pair(name):
            return pairs[JOB[name][0]]

        def filled(eng, name):
            p, n = JOB[name]
            eng.wait_ge(full[p], n + 1)
            return pairs[p]

        def emptied(eng, name):
            p, n = JOB[name]
            eng.wait_ge(free[p], n + 1)

        def drained(name):
            return free[JOB[name][0]]

        def head_job(head, b):
            p = 2 + b % 2
            return p, BEFORE_ROUTE[p] + b // 2 + 2 * head

        def flat(p, n=TOK):
            return p.rearrange("p a b -> p (a b)")[:, 0:n]

        def low(b):
            return wl[:, 1024 * b:1024 * b + 1024] if b < 3 else wl[:, 3072 + 512 * (b - 3):3584 + 512 * (b - 3)]

        def two(p):
            return p[:, :, 0:HT]

        def halves(v):
            return v.rearrange("p (a b) -> p a b", a=2)

        def utq(j):
            v = ut[:, j, :]
            return (v[:, 0:SEQ].rearrange("p (j c) -> p j c", j=L),
                    v[:, SEQ:].rearrange("p (t b) -> p t b", t=NT))

        def finish_act(act, t, rows):
            act.wait_ge(acc_ok, t + 1)
            if t:
                act.wait_ge(yt_out, 16 * t)
            act.activation(ytile[0:rows, :], h2[0:rows, t, :], ACT.Square, accum_out=fss[0:rows, :]).then_inc(fsq_ok, 1)
            act.wait_ge(fms_ok, t + 1)
            act.activation(frs[0:rows, :], frs[0:rows, :], ACT.Sqrt).then_inc(frt_ok, 1)

        @block.sync
        def _(sp):
            sp.dma_start(memT, a["mem_t"]).then_inc(mem_in, 16)
            sp.dma_start(nT, a["x_t"]).then_inc(x_in, 16)
            sp.dma_start(const, a["consts"]).then_inc(consts_in, 16)
            sp.dma_start(s5p, a["s5_pack"]).then_inc(s5_in, 16)

            def load(name, src, k=KD):
                s, n = LOAD[name]
                if n:
                    before = LOADED_BEFORE[name]
                    sp.wait_ge(full[before % 4], before // 4 + 1)
                sp.dma_start(wring[:, s, 0:k * P], src).then_inc(w_in[s], 16)

            for j in range(4):
                load(f"k{j}", a["w_mem_k"][j])
            for j in range(4):
                load(f"v{j}", a["w_mem_v"][j])
            sp.dma_start(h0.rearrange("p a b c -> p (a b c)"), a["h0"]).then_inc(h0_in, 16)
            for j in range(4):
                load(f"ag{j}", a["w_in"][8 + j])
                load(f"ai{j}", a["w_in"][4 + j])
            for j in range(4):
                load(f"u{j}", a["w_in"][j])
            for j in range(4):
                load(f"q{j}", a["w_in"][12 + j])
            filled(sp, "T")
            for n in range(2 * NB):
                if n >= 3:
                    sp.wait_ge(c_used[n % 3], n // 3)
                src = a["cache_k"][n] if n < NB else a["cache_v"][n - NB]
                sp.dma_start(cring[:, n % 3, :], src).then_inc(cin[n % 3], 16)
            for j in range(4):
                load(f"glu{j}", a["glu_w"][j], HALF)
            with sp.Fori(0, 4) as i:
                for r in range(2):
                    for b in range(6):
                        n = WGATE0 + 6 * r + b
                        s = n % WS
                        job = GATE0 + 6 * r + b - 6
                        sp.wait_ge(full[job % 4], job // 4 + 1 + 3 * i)
                        if b < 3:
                            sp.dma_start(wring[:, s, :], a["w_in"][bass.ds(16 + 8 * b + r + 2 * i, 1)]
                                         .rearrange("a p n -> (a p) n")).then_inc(w_in[s], 16)
                        else:
                            sp.dma_start(wring[:, s, 0:512], a["proj"][b - 3][bass.ds(r + 2 * i, 1)]
                                         .rearrange("a p n -> (a p) n")).then_inc(w_in[s], 16)
            for j in range(8):
                load(f"o{j}", a["w_out"][j])
                if j == 3:
                    job = GATE0 + 4 * LOOP_JOBS - 1
                    sp.wait_ge(full[job % 4], job // 4 + 1)
                    sp.dma_start(h2T, a["x_t"]).then_inc(x2_in, 16)
            for b in range(4):
                before = JOB_NUMBER[f"o{b + 2}"]
                sp.wait_ge(full[before % 4], before // 4 + 1)
                sp.dma_start(wring[:, b, :], a["peer_q"][b]).then_inc(w_in[b], 16)
            with sp.Fori(1, 4) as i:
                for b in range(4):
                    p, n = head_job(2 * i + b // 2 - 2, b % 2)
                    sp.wait_ge(full[p], n + 1)
                    sp.dma_start(wring[:, b, :], a["peer_q"][bass.ds(4 * i + b, 1)]
                                 .rearrange("a p n -> (a p) n")).then_inc(w_in[b], 16)
            p, n = head_job(PH - 1, 1)
            sp.wait_ge(full[p], n + 1)
            sp.dma_start(gf, a["final_g"].partition_broadcast(P)).then_inc(gf_in, 16)
            for t in range(TILES + 1):
                sp.wait_ge(yt_ok, t + 1)
                rows = P if t < TILES else NB * NT
                sp.dma_start(o["y"][t * P:t * P + rows, :], ytile[0:rows, :]).then_inc(yt_out, 16)
            sp.wait_ge(yt_out, 16 * (TILES + 1))
            sp.wait_ge(conv_out, 16 * (1 + HALF))
            sp.wait_ge(mem_out, 32)
            sp.wait_ge(state_out, 32)

        def loads_before_route(s):
            return (WROUTE0 - s + WS - 1) // WS

        @block.gpsimd
        def _(pool):
            pool.memset(ident, 0.0).then_inc(pool_step, 1)
            pool.wait_ge(pool_step, 1)
            pool.affine_select(out=ident, in_=ident, compare_op=ALU.not_equal, fill=1.0, base=0,
                               pattern=[[-1, P]], channel_multiplier=1).then_inc(made, 1)
            pool.memset(ones, 1.0).then_inc(made, 1)
            filled(pool, "ssm")
            pool.memset(Tm[:, 0:L - 1], 0.0).then_inc(t_zero, 1)
            filled(pool, "v")
            for j in range(HALF):
                pool.memset(ain[:, j, 0:PAD], 0.0).then_inc(pool_step, 1)
            hist = ain[:, :, ARUN:].rearrange("p c (b k) -> p c b k", b=NB)
            for j in range(HALF):
                pool.dma_start(hist[:, j, :, 0:PAD], a["conv_hist"][:, j]).then_inc(ain_zero, 16)
            pool.wait_ge(pool_step, 1 + HALF)
            pool.wait_ge(ain_zero, 16 * HALF)
            for j in range(HALF):
                emptied(pool, f"ai{j}")
                pool.tensor_tensor(ain[:, j, PAD:ARUN], ain[:, j, PAD:ARUN], sg[:, j % 2, 0:SEQ], ALU.mult)
                pool.tensor_tensor(hist[:, j, :, PAD:], hist[:, j, :, PAD:],
                                   sg[:, j % 2, SEQ:].rearrange("p (b t) -> p b t", b=NB),
                                   ALU.mult).then_inc(ain_ok, 1)
            pool.wait_ge(ain_ok, HALF)
            pool.dma_start(o["conv_p"], ain[:, :, SEQ:ARUN]).then_inc(conv_out, 16)
            for j in range(HALF):
                pool.dma_start(o["conv_s"][:, j], hist[:, j, :, NT:]).then_inc(conv_out, 16)
            emptied(pool, "u3")
            pool.dma_start(ubuf.rearrange("(q p) t -> p q t", p=P), ut).then_inc(ubuf_ok, 16)
            pool.wait_ge(epad_ok, 2)
            pool.memset(Us, 0.0).then_inc(us_zero, 1)
            pool.memset(Us2, 0.0).then_inc(us_zero, 1)
            pool.wait_ge(ubuf_ok, 16)
            pool.wait_ge(us_zero, 2)
            src = ubuf.rearrange("(g i) t -> i g t", i=CG)
            for j in range(L):
                pool.dma_start(U[CG * j:CG * (j + 1), :, :], src[:, :, NC * j:NC * (j + 1)]).then_inc(u_ok, 16)
            for j in range(NT):
                part = src[:, :, SEQ + NB * j:SEQ + NB * (j + 1)]
                pool.dma_start(Us[CG * j:CG * (j + 1), :, :], part).then_inc(u_ok, 16)
                pool.dma_start(Us2[64 + CG * j:64 + CG * (j + 1), :, :], part).then_inc(u_ok, 16)
            for n in ("k0", "k1", "k2", "k3", "v"):
                emptied(pool, n)
            pool.dma_start(o["mem_k"], kT).then_inc(mem_out, 16)
            pool.dma_start(o["mem_v"], vm).then_inc(mem_out, 16)
            for n in ("y0", "y1", "ys"):
                emptied(pool, n)
            dst = ybuf.rearrange("(g i) t -> i g t", i=CG)
            for j in range(L):
                pool.dma_start(dst[:, :, NC * j:NC * (j + 1)], Y[CG * j:CG * (j + 1), :, :]).then_inc(ybuf_ok, 16)
            for j in range(NT):
                pool.dma_start(dst[:, :, SEQ + NB * j:SEQ + NB * (j + 1)],
                               Ys[CG * j:CG * (j + 1), :, :]).then_inc(ybuf_ok, 16)
            pool.wait_ge(ybuf_ok, 16 * (L + NT))
            pool.dma_start(zg, ybuf.rearrange("(q p) t -> p q t", p=P)).then_inc(y_in, 16)
            pool.wait_ge(scan_ok, 1)
            pool.dma_start(o["ssm_p"], dve_t[:, 0, 0:G]).then_inc(state_out, 16)
            emptied(pool, "zs")
            pool.dma_start(o["ssm_s"], h0[:, 0]).then_inc(state_out, 16)
            filled(pool, "ss_o")
            pool.iota(iota16.bitcast(I32), pattern=[[1, TOPK]], base=0, channel_multiplier=0).then_inc(iota_ok, 1)

            def gather_u(n, par):
                pool.wait_ge(routed, n + 1)
                for j in range(TOPK):
                    first = isinstance(n, int) and n == 0 and j < RING
                    if not first:
                        pool.wait_ge(u_used, TOPK * n + (j - RING + 1))
                        pool.sem_inc(slot_free, 1)
                    pool.indirect_dma_start(uring[:, j % RING, :], None, a["peer_u"],
                                            bass.IndirectOffsetOnAxis(ap=idx_u[:, par, j:j + 1], axis=0)
                                            ).then_inc(u_in[j % RING], 16)

            def gather_v(n, par):
                pool.wait_ge(idxv_ok, n + 1)
                for j in range(TOPK):
                    first = isinstance(n, int) and n == 0 and j < RING
                    if not first:
                        pool.wait_ge(v_used, TOPK * n + (j - RING + 1))
                        pool.sem_inc(slot_free, 1)
                    pool.indirect_dma_start(vring[:, j % RING, :], None, a["peer_v"],
                                            bass.IndirectOffsetOnAxis(ap=idx_v[:, par, j:j + 1], axis=0)
                                            ).then_inc(v_in[j % RING], 16)

            gather_u(0, 0)
            gather_u(1, 1)
            for n in range(2):
                gather_u(n + LAG, n)
                gather_v(n, n)
            with pool.Fori(2, TILES * PH // 2) as i:
                for r in range(2):
                    gather_u(2 * i + r, r)
                    gather_v(2 * i + r - LAG, r)
            n = TOPK * TILES * PH
            pool.wait_ge(samples_routed, 1)
            for j in range(32):
                pool.wait_ge(u_used, n + j - RING + 1)
                pool.indirect_dma_start(uring[:, j % RING, :], None, a["peer_u"],
                                        bass.IndirectOffsetOnAxis(ap=idx_s[:, j:j + 1], axis=0)
                                        ).then_inc(u_in[j % RING], 16)
            for r in range(2):
                gather_v(TILES * PH - LAG + r, r)
            for j in range(32):
                pool.wait_ge(v_used, n + j - RING + 1)
                pool.indirect_dma_start(vring[:, j % RING, :], None, a["peer_v"],
                                        bass.IndirectOffsetOnAxis(ap=idx_s[:, j:j + 1], axis=0)
                                        ).then_inc(v_in[j % RING], 16)

        @block.tensor
        def _(pe):
            def begin(name):
                p, n = JOB[name]
                if n:
                    pe.wait_ge(free[p], n)
                return pairs[p]

            def loaded(name):
                s, n = LOAD[name]
                pe.wait_ge(w_in[s], 16 * (n + 1))
                return wring[:, s, :].rearrange("p (k m) -> p k m", m=P)

            def product(ps, w, rhs, k, ready=None):
                for j in range(k):
                    if ready is not None:
                        pe.wait_ge(ready, j + 1)
                    for h in range(2):
                        mm = pe.matmul(ps[:, h, 0:HT], w[:, j, :], rhs[:, j, h * HT:(h + 1) * HT],
                                       start=(j == 0), stop=(j == k - 1))
                return mm

            def split_product(ps, w, w_low, x, x_low, k, ready=None):
                for j in range(k):
                    if ready is not None:
                        pe.wait_ge(ready, j + 1)
                    for n, (wp, xp) in enumerate(((w, x), (w, x_low), (w_low, x))):
                        for h in range(2):
                            mm = pe.matmul(ps[:, h, 0:HT], wp[:, j * P:(j + 1) * P],
                                           xp[:, j, h * HT:(h + 1) * HT],
                                           start=(j == 0 and n == 0), stop=(j == k - 1 and n == 2))
                return mm

            def weighted(name, rhs, k=KD):
                w = loaded(name)
                ps = begin(name)
                product(ps, w, rhs, k).then_inc(full[JOB[name][0]], 1)

            pe.wait_ge(made, 2)
            ps = begin("ssm")
            for k in range(KD):
                pe.wait_ge(msq_ok, k + 1)
                mm = pe.matmul(ps[:, 0, 0:MEM], ones, msq[:, k, :], start=(k == 0), stop=(k == KD - 1))
            mm.then_inc(full[0], 1)
            ps = begin("ssx")
            for k in range(KD):
                pe.wait_ge(xsq_ok, k + 1)
                for h in range(2):
                    mm = pe.matmul(ps[:, h, 0:HT], ones, xsq[:, k, h * HT:(h + 1) * HT],
                                   start=(k == 0), stop=(k == KD - 1))
            mm.then_inc(full[1], 1)
            for j in range(4):
                w = loaded(f"k{j}")
                ps = begin(f"k{j}")
                for k in range(KD):
                    if j == 0:
                        pe.wait_ge(m_ok, k + 1)
                    mm = pe.matmul(ps[:, 0, 0:MEM], w[:, k, :], memT[:, k, :], start=(k == 0), stop=(k == KD - 1))
                mm.then_inc(full[JOB[f"k{j}"][0]], 1)
            ps = begin("v")
            for j in range(4):
                w = loaded(f"v{j}")
                for m in range(2):
                    for k in range(KD):
                        mm = pe.matmul(ps[:, m, j * P:(j + 1) * P], memT[:, k, m * P:(m + 1) * P], w[:, k, :],
                                       start=(k == 0), stop=(k == KD - 1))
            mm.then_inc(full[JOB["v"][0]], 1)
            pe.wait_ge(n_ok, KD)
            for j in range(4):
                weighted(f"ag{j}", nT)
                weighted(f"ai{j}", nT)
            for j in range(4):
                weighted(f"u{j}", nT)
            s5C = s5p[:, 3 * G + 2 * G * CG:3 * G + 3 * G * CG].rearrange("p (g i) -> p g i", g=G)
            pe.wait_ge(epad_ok, 2)
            ps = begin("T")
            for g in range(G):
                mm = pe.matmul(ps[:, 0, g * CG:(g + 1) * CG], Epad[:, g, 0:L, :].rearrange("p s i -> p (s i)"),
                               s5C[:, g, :], start=True, stop=True)
            mm.then_inc(full[JOB["T"][0]], 1)
            for b in range(4):
                ps = flat(begin(f"ET{b}"), 1024).rearrange("p (g n) -> p g n", g=8)
                for g in range(8):
                    mm = pe.transpose(ps[:, g, :], Epad[:, 8 * b + g, 0:L, :].rearrange("p s i -> p (s i)"), ident)
                mm.then_inc(full[JOB[f"ET{b}"][0]], 1)
            for j in range(2):
                weighted(f"q{j}", nT)
            pe.wait_ge(u_ok, 16 * (L + 2 * NT))
            for b in range(4):
                emptied(pe, f"ET{b}")
            for e in range(2):
                for h in range(2):
                    ps = flat(begin(f"z{e}{h}"), 1024).rearrange("p (g n) -> p g n", g=16)
                    for g in range(16):
                        mm = pe.matmul(ps[:, g, :], ET[:, 16 * h + g, 64 * e:64 * e + P], U[:, 16 * h + g, :],
                                       start=True, stop=True)
                    mm.then_inc(full[JOB[f"z{e}{h}"][0]], 1)
            for j in range(2, 4):
                weighted(f"q{j}", nT)

            for n in ("q0", "q1", "q2", "q3", "k0", "k1", "k2", "k3", "v"):
                emptied(pe, n)
            ps = begin("ss_s")
            for b in range(NB):
                pe.wait_ge(cin[b % 3], 16 * (b // 3 + 1))
                kc = cring[:, b % 3, :].rearrange("p (h m) -> p h m", h=HEADS)
                for h in range(HEADS):
                    for m in range(2):
                        mm = pe.matmul(ps[:, 0, m * P + 16 * b + 4 * h:m * P + 16 * b + 4 * h + NT],
                                       kc[:, h, m * P:(m + 1) * P], qT[:, h, SEQ + NT * b:SEQ + NT * (b + 1)],
                                       start=True, stop=True)
                if b < NB - 1:
                    mm.then_inc(c_used[b % 3], 1)
            mm.then_inc(full[JOB["ss_s"][0]], 1)
            pe.wait_ge(full[JOB["ss_s"][0]], JOB["ss_s"][1] + 1)
            pe.sem_inc(c_used[(NB - 1) % 3], 1)
            def within(gg):
                return Tm.rearrange("p i o g -> p (i o) g")[:, :, gg]

            def from_state(gg):
                return CL[:, gg, :, :].rearrange("p i o -> p (i o)")

            pe.wait_ge(h0_in, 16)
            pe.wait_ge(t_in, 16 * (L - 1))
            emptied(pe, "T")
            ps = begin("ys")
            for g in range(G):
                pe.matmul(ps[:, 0, NB * g:NB * (g + 1)], within(g), Us[:, g, :], start=True, stop=False)
                mm = pe.matmul(ps[:, 0, NB * g:NB * (g + 1)], from_state(g), h0[:, 0, g, :], start=False, stop=True)
            mm.then_inc(full[JOB["ys"][0]], 1)
            ps = begin("zs")
            for g in range(G):
                mm = pe.matmul(ps[:, 0, NB * g:NB * (g + 1)], ET[:, g, 0:P], Us2[:, g, :], start=True, stop=True)
            mm.then_inc(full[JOB["zs"][0]], 1)
            def channel_sums(name, src):
                ps = begin(name)
                for k in range(HALF):
                    if src is lsq:
                        pe.wait_ge(lsq_ok, k + 1)
                    for h in range(2):
                        mm = pe.matmul(ps[:, h, 0:HT], ones, src[:, k, h * HT:(h + 1) * HT],
                                       start=(k == 0), stop=(k == HALF - 1))
                mm.then_inc(full[JOB[name][0]], 1)

            pe.wait_ge(conv_step, TAPS * HALF + 2 * TAPS)
            channel_sums("lnm", cact)

            pe.wait_ge(scan_ok, 1)
            for h in range(2):
                ps = flat(begin(f"y{h}"), 1024).rearrange("p (g n) -> p g n", g=16)
                for g in range(16):
                    gg = 16 * h + g
                    pe.matmul(ps[:, g, :], within(gg), U[:, gg, :], start=True, stop=False)
                    mm = pe.matmul(ps[:, g, :], from_state(gg), Z[:, 0, gg, 0:NC], start=False, stop=True)
                mm.then_inc(full[JOB[f"y{h}"][0]], 1)
            def scores(t):
                ps = flat(begin(f"as{t}"), 1024).rearrange("p (h m) -> p h m", h=HEADS)
                for h in range(HEADS):
                    mm = pe.matmul(ps[:, h, :], qT[:, h, t * P:(t + 1) * P], kT[:, h, :], start=True, stop=True)
                mm.then_inc(full[JOB[f"as{t}"][0]], 1)

            def turn(t):
                pe.wait_ge(p_ok, t + 1)
                ps = flat(begin(f"at{t}"), 1024).rearrange("p (h c m) -> p h c m", h=HEADS, c=2)
                for h in range(HEADS):
                    for m in range(2):
                        mm = pe.transpose(ps[:, h, m, :], Pm[:, h, m * P:(m + 1) * P], ident)
                mm.then_inc(full[JOB[f"at{t}"][0]], 1)

            def values(t):
                emptied(pe, f"at{t}")
                ps = begin(f"ao{t}")
                for h in range(HEADS):
                    for m in range(2):
                        mm = pe.matmul(ps[:, 0, h * P:(h + 1) * P], vm[:, m, h * P:(h + 1) * P], PT[:, h, m, :],
                                       start=(m == 0), stop=(m == 1))
                mm.then_inc(full[JOB[f"ao{t}"][0]], 1)

            scores(0)
            for t in range(TILES):
                if t + 1 < TILES:
                    scores(t + 1)
                if t == 0:
                    channel_sums("lnv", lsq)
                turn(t)
                values(t)
            ps = begin("ss_t")
            emptied(pe, "ss_s")
            for m in range(2):
                mm = pe.transpose(ps[:, 0, m * P:(m + 1) * P], ST[:, m, :], ident)
            mm.then_inc(full[JOB["ss_t"][0]], 1)
            ps = begin("ss_p")
            pe.wait_ge(p_ok, TILES + 1)
            for m in range(2):
                mm = pe.transpose(ps[:, 0, m * P:(m + 1) * P], Ps[:, m * P:(m + 1) * P], ident)
            mm.then_inc(full[JOB["ss_p"][0]], 1)
            ps = begin("ss_o")
            emptied(pe, "ss_p")
            for b in range(NB):
                n = NB + b
                pe.wait_ge(cin[n % 3], 16 * (n // 3 + 1))
                vc = cring[:, n % 3, :].rearrange("p (c n) -> p c n", c=2)
                for h in range(HEADS):
                    for m in range(2):
                        mm = pe.matmul(ps[:, 0, 32 * h + NT * b:32 * h + NT * (b + 1)], vc[:, m, h * P:(h + 1) * P],
                                       PTs[:, m, 16 * b + 4 * h:16 * b + 4 * h + NT],
                                       start=(m == 0), stop=(m == 1))
                if b < NB - 1:
                    mm.then_inc(c_used[n % 3], 1)
            mm.then_inc(full[JOB["ss_o"][0]], 1)
            pe.wait_ge(zz_ok, HALF)
            for j in range(4):
                weighted(f"glu{j}", zz, HALF)
            emptied(pe, "ao3")
            emptied(pe, "ss_o")
            pe.wait_ge(nl_ok, KD)
            with pe.Fori(0, 4) as i:
                for r in range(2):
                    for b in range(6):
                        job, ld = GATE0 + 6 * r + b, WGATE0 + 6 * r + b
                        p, s = job % 4, ld % WS
                        pe.wait_ge(w_in[s], 16 * (ld // WS + 1) + 32 * i)
                        pe.wait_ge(free[p], job // 4 + 3 * i)
                        if b == 3:
                            pe.wait_ge(bl_ok, 3 * HALF)
                        pe.wait_ge(wl_ok, 6 * r + b + 1 + 12 * i)
                        x, x_low = ((nTh, nTl) if b < 3 else ((zh, zl), (ch, cl), (qh, ql))[b - 3])
                        mm = split_product(pairs[p], whigh[:, s, :], low(b), x, x_low, KD if b < 3 else HALF)
                        mm.then_inc(full[p], 1)
            for j in range(8):
                loaded(f"o{j}")
                ps = begin(f"o{j}")
                pe.wait_ge(wl_ok, 48 + j + 1)
                split_product(ps, whigh[:, LOAD[f"o{j}"][0], :], wl[:, 1024 * (j % 4):1024 * (j % 4) + 1024],
                              mh, ml, KD, ml_ok if j == 0 else None).then_inc(full[JOB[f"o{j}"][0]], 1)
            ps = begin("ss2")
            for k in range(KD):
                pe.wait_ge(h2sq_ok, k + 1)
                for h in range(2):
                    mm = pe.matmul(ps[:, h, 0:HT], ones, h2sq[:, k, h * HT:(h + 1) * HT],
                                   start=(k == 0), stop=(k == KD - 1))
            mm.then_inc(full[JOB["ss2"][0]], 1)
            for t in range(TILES + 1):
                ps = flat(begin(f"ht{t}"), 1024)
                rows = P if t < TILES else NB * NT
                for k in range(KD):
                    mm = pe.transpose(ps[0:rows, k * P:(k + 1) * P], h2T[:, k, t * P:t * P + rows], ident)
                mm.then_inc(full[JOB[f"ht{t}"][0]], 1)
            keys = c("keys", 0, 256).rearrange("p (s k) -> p s k", s=2)
            def head_products(i, r):
                for b in range(4):
                    p, n = head_job(2 * i + r, b)
                    pe.wait_ge(free[p], n)
                    if b < 2:
                        s = 2 * r + b
                        pe.wait_ge(w_in[s], 16 * (loads_before_route(s) + 1) + 16 * i)
                        w = wring[:, s, :].rearrange("p (k m) -> p k m", m=P)
                        first = isinstance(i, int) and (i, r, b) == (0, 0, 0)
                        mm = product(pairs[p], w, xbT, KD, xbT_ok if first else None)
                        mm.then_inc(full[p], 1)
                    else:
                        pq, n = head_job(2 * i + r, b - 2)
                        pe.wait_ge(free[pq], n + 1)
                        for t in range(TILES + 1):
                            mm = pe.matmul(flat(pairs[p], 640)[:, t * P:(t + 1) * P],
                                           qbuf[:, b - 2, t * P:(t + 1) * P], keys[:, b - 2, :],
                                           start=True, stop=True)
                        mm.then_inc(full[p], 1)

            def sum_v(n, par):
                if not (isinstance(n, int) and n < 2):
                    pe.wait_ge(acc_step, n - 1)
                for j in range(TOPK):
                    pe.wait_ge(v_in[j % RING], 32 * n + 16 * (j // RING + 1))
                    pe.wait_ge(diag_ok, TOPK * n + j + 1)
                    for h in range(2):
                        mm = pe.matmul(pairs[par][:, h, :], diag[:, j % RING, :],
                                       vring[:, j % RING, h * 512:(h + 1) * 512],
                                       start=(j == 0), stop=(j == TOPK - 1))
                    mm.then_inc(v_used, 1)

            head_products(0, 0)
            for t in range(TILES + 1):
                ps = flat(begin(f"xt{t}"), 1024)
                for k in range(KD):
                    mm = pe.transpose(ps[:, k * P:(k + 1) * P], xbT[:, k, t * P:(t + 1) * P], ident)
                mm.then_inc(full[JOB[f"xt{t}"][0]], 1)
            for head in range(1, 4):
                head_products(head // 2, head % 2)
            for p in range(2):
                pe.wait_ge(free[p], BEFORE_ROUTE[p] + (TILES + 2 - p) // 2)
            for head in range(4, PH):
                head_products(head // 2, head % 2)
                sum_v(head - 4, head % 2)
            with pe.Fori(2, TILES * PH // 2) as i:
                sum_v(2 * i, 0)
                sum_v(2 * i + 1, 1)
            n = TOPK * TILES * PH
            pe.wait_ge(acc_step, TILES * PH - 1)
            for j in range(32):
                pe.wait_ge(v_in[j % RING], 16 * (2 * TILES * PH + j // RING + 1))
                pe.wait_ge(diag_ok, n + j + 1)
                for h in range(2):
                    mm = pe.matmul(pairs[0][0:32, h, :], diag[:, j % RING, 0:32],
                                   vring[:, j % RING, h * 512:(h + 1) * 512], start=(j == 0), stop=(j == 31))
                mm.then_inc(v_used, 1)

        @block.scalar
        def _(act):
            act.wait_ge(mem_in, 16)
            for k in range(KD):
                act.activation(msq[:, k, :], memT[:, k, :], ACT.Square).then_inc(msq_ok, 1)
            act.wait_ge(x_in, 16)
            for k in range(KD):
                act.activation(xsq[:, k, :], nT[:, k, :], ACT.Square).then_inc(xsq_ok, 1)
            emptied(act, "ssm")
            act.activation(mr, mr, ACT.Sqrt).then_inc(rms_ok, 1)
            emptied(act, "ssx")
            act.activation(xr, xr, ACT.Sqrt).then_inc(rms_ok, 1)
            act.wait_ge(s5_in, 16)
            act.activation(at(tab, G), s5p[:, 0:G], ACT.Tanh, scale=1.0 / 16).then_inc(s5_scan_in, 1)
            for j in range(4):
                ps = filled(act, f"k{j}")
                act.activation(kT[:, j, :], ps[:, 0, 0:MEM], ACT.Copy).then_inc(drained(f"k{j}"), 1)
            act.wait_ge(epad_ok, 1)
            act.activation(at(tab + 288 * 2, 288), at(tab + 288 * 2, 288), ACT.Tanh, scale=0.5).then_inc(s5_scan_in, 1)
            act.activation(at(tab + 288 * 3, 288), at(tab, 288), ACT.Sin)
            act.activation(at(tab + 288 * 4, 288), at(tab + 288, 288), ACT.Sin)
            act.activation(at(tab + 2304, G), at(tab + 2304, G), ACT.Sin, scale=0.5).then_inc(s5_scan_in, 1)
            act.wait_ge(consts_in, 16)
            ps = filled(act, "v")
            act.activation(vm.rearrange("p a b -> p (a b)"), flat(ps, 1024), ACT.Copy).then_inc(drained("v"), 1)
            hist = ain[:, :, ARUN:].rearrange("p c (b k) -> p c b k", b=NB)
            for j in range(4):
                ps = filled(act, f"ag{j}")
                if j >= 2:
                    act.wait_ge(ain_ok, j - 1)
                act.activation(halves(sg[:, j % 2, :]), two(ps), ACT.Sigmoid, bias=c("b_in", 8 + j)
                               ).then_inc(drained(f"ag{j}"), 1)
                ps = filled(act, f"ai{j}")
                act.activation(ain[:, j, PAD:PAD + HT], ps[:, 0, 0:HT], ACT.Identity, bias=c("b_in", 4 + j))
                act.activation(ain[:, j, PAD + HT:ARUN], ps[:, 1, 0:SEQ - HT], ACT.Identity, bias=c("b_in", 4 + j))
                act.activation(hist[:, j, :, PAD:], ps[:, 1, SEQ - HT:HT].rearrange("p (b t) -> p b t", b=NB),
                               ACT.Identity, bias=c("b_in", 4 + j)).then_inc(drained(f"ai{j}"), 1)
            for j in range(4):
                ps = filled(act, f"u{j}")
                dst = utq(j)
                act.activation(dst[0][:, :, 0:HT // L], ps[:, 0, 0:HT].rearrange("p (c j) -> p j c", j=L),
                               ACT.Identity, bias=c("b_in", j))
                act.activation(dst[0][:, :, HT // L:NC], ps[:, 1, 0:SEQ - HT].rearrange("p (c j) -> p j c", j=L),
                               ACT.Identity, bias=c("b_in", j))
                act.activation(dst[1], ps[:, 1, SEQ - HT:HT].rearrange("p (b t) -> p t b", b=NB),
                               ACT.Identity, bias=c("b_in", j)).then_inc(drained(f"u{j}"), 1)
            ps = filled(act, "T")
            last = Tm[:, L - 1]
            act.activation(last, ps[:, 0, :].rearrange("p (g o) -> p o g", g=G), ACT.Copy).then_inc(drained("T"), 1)
            act.wait_ge(t_zero, 1)
            emptied(act, "T")
            for i in range(L - 1):
                act.dma_start(Tm[0:CG * (i + 1), i], last[CG * (L - 1 - i):, :]).then_inc(t_in, 16)
            for b in range(4):
                if b == 2:
                    act.wait_ge(ubuf_ok, 16)
                ps = flat(filled(act, f"ET{b}"), 1024).rearrange("p (g n) -> p g n", g=8)
                act.activation(ET[:, 8 * b:8 * b + 8, 0:P], ps, ACT.Copy)
                act.activation(ET[:, 8 * b:8 * b + 8, P:], ps[:, :, 0:64], ACT.Copy).then_inc(drained(f"ET{b}"), 1)
            def query(j):
                ps = filled(act, f"q{j}")
                act.activation(halves(qT[:, j, :]), two(ps), ACT.Identity, bias=c("b_in", 12 + j)
                               ).then_inc(drained(f"q{j}"), 1)

            query(0)
            query(1)
            for e in range(2):
                for h in range(2):
                    ps = flat(filled(act, f"z{e}{h}"), 1024).rearrange("p (g n) -> p g n", g=16)
                    act.activation(Z[:, e, 16 * h:16 * h + 16, 1:], ps, ACT.Copy).then_inc(drained(f"z{e}{h}"), 1)
            query(2)
            query(3)
            ps = filled(act, "ss_s")
            act.activation(ST.rearrange("p a b -> p (a b)"), ps[:, 0, 0:MEM], ACT.Copy).then_inc(drained("ss_s"), 1)
            act.wait_ge(conv_out, 16 * (1 + HALF))
            for j in range(HALF):
                if j < HALF - 1:
                    act.wait_ge(lnx_ok, j + 1)
                else:
                    emptied(act, "lnm")
                act.activation(lsq[:, j, :], cact[:, j, :], ACT.Square).then_inc(lsq_ok, 1)
            scale = float(P) ** -0.5
            for t in range(TILES):
                ps = flat(filled(act, f"as{t}"), 1024).rearrange("p (h m) -> p h m", h=HEADS)
                act.wait_ge(max_ok, t + 1)
                for h in range(HEADS):
                    ins = act.activation(Pm[:, h, :], ps[:, h, :], ACT.Exp, bias=nmx[:, h:h + 1], scale=scale,
                                         accum_out=asum[:, h:h + 1])
                ins.then_inc(drained(f"as{t}"), 1)
                if t == 0:
                    emptied(act, "lnv")
                    act.activation(lrs, lrs, ACT.Sqrt).then_inc(lr_ok, 1)
                ps = filled(act, f"at{t}")
                act.activation(PT.rearrange("p h c m -> p (h c m)"), flat(ps, 1024), ACT.Copy
                               ).then_inc(drained(f"at{t}"), 1)
                ps = filled(act, f"ao{t}")
                act.activation(qT[:, :, t * P:(t + 1) * P], ps[:, 0, :].rearrange("p (h t) -> p h t", h=HEADS),
                               ACT.Copy).then_inc(drained(f"ao{t}"), 1)
            for j in range(HALF):
                act.wait_ge(lnx_ok, HALF + j)
                act.activation(cact[:, j, :], cact[:, j, :], ACT.Silu, bias=c("lb", j)).then_inc(cact_ok, 1)
            ps = filled(act, "ss_t")
            act.wait_ge(max_ok, TILES + 1)
            act.activation(Ps, ps[:, 0, 0:MEM], ACT.Exp, bias=nmx[:, 0:1], scale=scale, accum_out=asum[:, 0:1]
                           ).then_inc(drained("ss_t"), 1)
            ps = filled(act, "ss_p")
            act.activation(PTs.rearrange("p a b -> p (a b)"), ps[:, 0, 0:MEM], ACT.Copy).then_inc(drained("ss_p"), 1)
            act.wait_ge(y_in, 16)
            for j in range(HALF):
                act.activation(zz[:, j, 0:SEQ].rearrange("p (c i) -> p i c", i=L),
                               zg[:, j, 0:SEQ].rearrange("p (i c) -> p i c", i=L), ACT.Gelu)
                act.activation(zz[:, j, SEQ:].rearrange("p (b t) -> p t b", b=NB),
                               zg[:, j, SEQ:].rearrange("p (t b) -> p t b", b=NB), ACT.Gelu).then_inc(zz_ok, 1)
            ps = filled(act, "ss_o")
            act.activation(qT[:, :, SEQ:], ps[:, 0, 0:P].rearrange("p (h t) -> p h t", h=HEADS), ACT.Copy
                           ).then_inc(drained("ss_o"), 1)
            act.wait_ge(zz_ok, HALF)
            for j in range(4):
                ps = filled(act, f"glu{j}")
                act.activation(halves(zg[:, j, :]), two(ps), ACT.Sigmoid, bias=c("glu_b", j)
                               ).then_inc(drained(f"glu{j}"), 1)
            act.wait_ge(mem_out, 32)
            with act.Fori(0, 4) as i:
                for r in range(2):
                    for b in range(3):
                        job = GATE0 + 6 * r + b
                        act.wait_ge(full[job % 4], job // 4 + 1 + 3 * i)
                        act.wait_ge(merged_ok, 2 * r + 4 * i)
                        act.activation(halves(gsg[:, r, b, :]), two(pairs[job % 4]), ACT.Sigmoid,
                                       bias=const[:, bass.ds(16 + 8 * b + r + 2 * i, 1)]
                                       ).then_inc(free[job % 4], 1)
            for k in range(KD):
                emptied(act, f"o{k}")
                act.activation(h2sq[:, k, :], h2T[:, k, :], ACT.Square).then_inc(h2sq_ok, 1)
            emptied(act, "ss2")
            act.activation(h2r, h2r, ACT.Sqrt).then_inc(h2r_ok, 1)
            for t in range(TILES + 1):
                ps = filled(act, f"ht{t}")
                rows = P if t < TILES else NB * NT
                act.activation(h2[0:rows, t, :], flat(ps, 1024)[0:rows, :], ACT.Copy).then_inc(drained(f"ht{t}"), 1)
            def queries(head):
                for b in range(4):
                    p, n = head_job(head, b)
                    ps = pairs[p]
                    act.wait_ge(full[p], n + 1)
                    if b < 2:
                        act.activation(halves(qbuf[:, b, 0:TOK]), two(ps), ACT.Copy)
                        act.activation(qbuf[:, b, TOK:].rearrange("p (r t) -> p r t", r=3),
                                       ps[:, 1, SEQ - HT:HT].unsqueeze(1).to_broadcast([P, 3, 32]),
                                       ACT.Copy).then_inc(free[p], 1)
                    else:
                        v = sc.rearrange("p (t h) s k -> p t h s k", t=5)
                        act.activation(v[:, :, head, b - 2, :],
                                       flat(ps, 640).rearrange("p (t k) -> p t k", t=5),
                                       ACT.Copy).then_inc(free[p], 1)

            def exp_of(n):
                act.wait_ge(cdiff, n + 1)
                act.activation(ce, cv, ACT.Exp, accum_out=esum).then_inc(cexp, 1)

            def gelu_of(n, par):
                act.wait_ge(u_used, TOPK * n + TOPK)
                act.activation(gel[:, par, :], dots[:, par, :], ACT.Gelu).then_inc(gel_ok, 1)

            def diags(n, lo, hi):
                for j in range(lo, hi):
                    if not (isinstance(n, int) and n == 0 and j < RING):
                        act.wait_ge(v_used, TOPK * n + (j - RING + 1))
                    act.activation(diag[:, j % RING, :], ident, ACT.Copy,
                                   scale=gate.rearrange("p a b -> p (a b)")[:, bass.ds(TOPK * n + j, 1)]
                                   ).then_inc(diag_ok, 1)

            def step(n, r, first, count=1, head=None):
                lagging = not (isinstance(n, int) and n < LAG)
                if lagging:
                    act.wait_ge(w_ok, n - LAG + 1)
                    diags(n - LAG, 0, RING)
                if head is not None:
                    queries(head)
                gelu_of(n, r)
                if count:
                    exp_of(first)
                if lagging:
                    diags(n - LAG, RING, TOPK)
                if count == 2:
                    exp_of(first + 1)

            for n in range(LAG):
                queries(n)
                for t in range((TILES + 1) * (n == 0)):
                    ps = filled(act, f"xt{t}")
                    act.activation(xb[:, t, :], flat(ps, 1024), ACT.Copy).then_inc(drained(f"xt{t}"), 1)
                exp_of(n)
            for n in range(PH):
                step(n, n % 2, n + LAG, head=n + LAG if n + LAG < PH else None)
            for t, first, count in ((1, lambda n: n + LAG, 1), (2, lambda n: 2 * n + LAG - 2 * PH, 2),
                                    (3, lambda n: n + LAG + PH, 1)):
                for n in range(PH * t, PH * t + 4):
                    step(n, n % 2, first(n), count)
                    if n == PH * t + LAG:
                        finish_act(act, t - 1, P)
                with act.Fori(4 * t + 2, 4 * t + 4 - (t == 3)) as i:
                    for r in range(2):
                        step(2 * i + r, r, first(2 * i + r), count)
            for r in range(2):
                step(TILES * PH - LAG + r, r, 0, 0)
            diags(30, 0, RING)
            n = TOPK * TILES * PH
            act.wait_ge(u_used, n + 32)
            act.activation(gel.rearrange("p a b -> p (a b)"), dots.rearrange("p a b -> p (a b)"), ACT.Gelu
                           ).then_inc(gel_ok, 1)
            diags(30, RING, TOPK)
            diags(31, 0, TOPK)
            act.wait_ge(w_ok, TILES * PH + 1)
            for j in range(32):
                if j == RING:
                    finish_act(act, TILES - 1, P)
                act.wait_ge(v_used, n + j - RING + 1)
                act.activation(diag[:, j % RING, 0:32], fold, ACT.Copy, scale=gate_s[:, j:j + 1]).then_inc(diag_ok, 1)
            finish_act(act, TILES, NB * NT)

        @block.vector
        def _(dve):
            steps = [0]

            def link(ins):
                steps[0] += 1
                ins.then_inc(dve_step, 1)
                dve.wait_ge(dve_step, steps[0])

            tt, ts, stt = dve.tensor_tensor, dve.tensor_scalar, dve.scalar_tensor_tensor
            ps = filled(dve, "ssm")
            ts(mr, ps[:, 0, 0:MEM], 1.0 / D, RMS_EPS, ALU.mult, ALU.add).then_inc(free[0], 1)
            dve.wait_ge(consts_in, 16)
            dve.wait_ge(rms_ok, 1)
            link(dve.reciprocal(mr, mr))
            for k in range(KD):
                stt(memT[:, k, :], memT[:, k, :], c("gm", k), mr, ALU.mult, ALU.mult).then_inc(m_ok, 1)
            ps = filled(dve, "ssx")
            ts(halves(xr), two(ps), 1.0 / D, RMS_EPS, ALU.mult, ALU.add).then_inc(free[1], 1)
            dve.wait_ge(rms_ok, 2)
            link(dve.reciprocal(xr, xr))
            for k in range(KD):
                stt(nT[:, k, :], nT[:, k, :], c("g1", k), xr, ALU.mult, ALU.mult).then_inc(n_ok, 1)
            W = 9 * G

            def tb(i):
                return at(tab + 288 * i, 9, G)

            dt = at(tab + 2336, G)
            one = at(tab + 2368, G)
            two_ = at(tab + 2400, G)
            three = at(tab + 2432, G)
            four = at(tab + 2464, G)
            five = at(tab + 2496, G)
            a_re, a_im = s5p[:, G:2 * G], s5p[:, 2 * G:3 * G]
            link(dve.memset(sgn[0:64, :], -1.0))
            link(dve.memset(sgn[64:P, :], 1.0))
            dve.wait_ge(s5_in, 16)
            dve.wait_ge(s5_scan_in, 1)
            link(ts(one, at(tab, G), -1.0, 1.0, ALU.mult, ALU.add))
            link(dve.reciprocal(two_, one))
            link(ts(one, at(tab, G), 1.0, None, ALU.add))
            link(tt(dt, one, two_, ALU.mult))
            for _ in range(3):
                link(tt(dt, dt, dt, ALU.mult))
            link(tt(one, a_im, dt, ALU.mult))
            link(tt(two_, a_re, dt, ALU.mult))
            for s in range(9):
                link(ts(tb(0)[:, s, :], one, float(8 - s), None, ALU.mult))
                link(ts(tb(2)[:, s, :], two_, float(8 - s), None, ALU.mult))
            th, ki, q1 = at(tab, W), at(tab + 288, W), at(tab + 288 * 5, W)
            link(ts(q1, th, 1.0 / (2 * PI), None, ALU.mult))
            link(dve.tensor_copy(ki.bitcast(I32), q1))
            link(dve.tensor_copy(q1, ki.bitcast(I32)))
            link(stt(th, q1, -TWO_PI_HI, th, ALU.mult, ALU.add))
            link(stt(th, q1, -TWO_PI_LO, th, ALU.mult, ALU.add))
            link(ts(th, th, -PI, PI, ALU.max, ALU.min))
            link(ts(q1, th, -1.0, None, ALU.mult))
            link(tt(q1, q1, th, ALU.max))
            link(ts(at(tab + 288, W), q1, -1.0, PI / 2, ALU.mult, ALU.add))
            link(dve.tensor_copy(at(tab + 2304, G), tb(0)[:, 7, :]))
            dve.sem_inc(epad_ok, 1)
            dve.wait_ge(s5_scan_in, 3)
            t_, m_, sn, cs = tb(2), tb(5), tb(3), tb(4)
            link(ts(m_, t_, -1.0, 1.0, ALU.mult, ALU.add))
            link(dve.reciprocal(tb(6), m_))
            link(ts(m_, t_, 1.0, None, ALU.add))
            link(tt(m_, m_, tb(6), ALU.mult))
            em1 = three
            link(stt(em1, t_[:, 7, :], 2.0, tb(6)[:, 7, :], ALU.mult, ALU.mult))
            link(tt(em1, em1, cs[:, 7, :], ALU.mult))
            half = at(tab + 2304, G)
            link(tt(half, half, half, ALU.mult))
            nr, ni = em1, four
            link(stt(nr, half, -2.0, em1, ALU.mult, ALU.add))
            link(tt(tb(0), m_, cs, ALU.mult))
            link(tt(tb(1), m_, sn, ALU.mult))
            Lre, Lim = tb(0), tb(1)
            link(dve.tensor_copy(ni, Lim[:, 7, :]))
            link(tt(one, a_re, a_re, ALU.mult))
            link(tt(two_, a_im, a_im, ALU.mult))
            link(tt(one, one, two_, ALU.add))
            link(dve.reciprocal(two_, one))
            link(tt(one, nr, a_re, ALU.mult))
            link(tt(five, ni, a_im, ALU.mult))
            link(tt(one, one, five, ALU.add))
            link(tt(one, one, two_, ALU.mult))
            link(tt(five, ni, a_re, ALU.mult))
            link(tt(nr, nr, a_im, ALU.mult))
            link(tt(five, five, nr, ALU.subtract))
            link(tt(two_, five, two_, ALU.mult))
            fr = one.unsqueeze(1).to_broadcast([P, 8, G])
            fi = two_.unsqueeze(1).to_broadcast([P, 8, G])
            g1, g2, gt = tb(2)[:, 1:, :], tb(3)[:, 1:, :], tb(4)[:, 1:, :]
            link(tt(g1, Lre[:, 1:, :], fr, ALU.mult))
            link(tt(gt, Lim[:, 1:, :], fi, ALU.mult))
            link(tt(g1, g1, gt, ALU.subtract))
            link(tt(g2, Lim[:, 1:, :], fr, ALU.mult))
            link(tt(gt, Lre[:, 1:, :], fi, ALU.mult))
            link(tt(g2, g2, gt, ALU.add))
            link(ts(g2, g2, sgn[:, 0:1], None, ALU.mult))
            s5B = s5p[:, 3 * G:3 * G + 2 * G * CG].rearrange("p (a g i) -> p a g i", a=2, g=G)
            s5C = s5p[:, 3 * G + 2 * G * CG:].rearrange("p (a g i) -> p a g i", a=2, g=G)
            link(dve.memset(Epad[:, :, L:, :], 0.0))
            tmp = CL.rearrange("p g s i -> p (g s i)").rearrange("p (s x) -> p s x", s=L)

            def bs(v):
                return v.rearrange("p g i -> p (g i)").rearrange("p (g i) -> p g i", i=CG)

            for s in range(L):
                e = Epad[:, :, s, :]
                t1 = tmp[:, s, :].rearrange("p (g i) -> p g i", i=CG)
                tt(t1, s5B[:, 1], g2[:, s, :].unsqueeze(2).to_broadcast([P, G, CG]), ALU.mult)
                link(tt(e, s5B[:, 0], g1[:, s, :].unsqueeze(2).to_broadcast([P, G, CG]), ALU.mult))
                link(tt(e, e, t1, ALU.add))
            h1, h2_ = tb(2)[:, 0:8, :], tb(3)[:, 0:8, :]
            link(ts(h1, Lre[:, 0:8, :], sgn[:, 0:1], -1.0, ALU.mult, ALU.mult))
            link(ts(h2_, Lim[:, 0:8, :], -1.0, None, ALU.mult))
            ct = at(tab + 288 * 4, G, CG)
            for i in range(L):
                s = L - 1 - i
                e = CL[:, :, i, :]
                tt(ct, s5C[:, 1], h2_[:, s, :].unsqueeze(2).to_broadcast([P, G, CG]), ALU.mult)
                link(tt(e, s5C[:, 0], h1[:, s, :].unsqueeze(2).to_broadcast([P, G, CG]), ALU.mult))
                link(tt(e, e, ct, ALU.add))
            link(ts(s5C[:, 0], s5C[:, 0], sgn[:, 0:1], -1.0, ALU.mult, ALU.mult))
            for e in range(2):
                link(dve.tensor_copy(A8[:, e, :], Lre[:, 0, :]))
            link(ts(B8[:, 0, :], Lim[:, 0, :], sgn[:, 0:1], None, ALU.mult))
            link(ts(B8[:, 1, :], B8[:, 0, :], -1.0, None, ALU.mult))
            link(dve.tensor_copy(A4, Lre[:, 4, :]))
            link(ts(B4, Lim[:, 4, :], sgn[:, 0:1], None, ALU.mult))
            dve.sem_inc(epad_ok, 1)
            acol = ain.rearrange("p c n -> p (c n)")
            ccol = cact.rearrange("p c n -> p (c n)")
            with dve.Fori(0, HALF // 2) as i:
                dve.wait_ge(ain_ok, 2 * i + 2)
                for k in range(TAPS):
                    for r in range(2):
                        j, n = 2 * i + r, 2 * k + r
                        w = const[:, bass.ds(COLS["cw"][0] + k + TAPS * j, 1)]
                        v, src = ccol[:, bass.ds(TOK * j, SEQ)], acol[:, bass.ds(AIN * j + k, SEQ)]
                        if k == 0:
                            ts(v, src, w, const[:, bass.ds(COLS["cb"][0] + j, 1)], ALU.mult, ALU.add
                               ).then_inc(conv_step, 1)
                        else:
                            dve.wait_ge(conv_step, n - 1 + 2 * TAPS * i)
                            stt(v, src, w, v, ALU.mult, ALU.add).then_inc(conv_step, 1)
            hist = ain[:, :, ARUN:].rearrange("p c (b k) -> p c b k", b=NB)
            taps = c("cw", 0, HALF * TAPS).rearrange("p (c k) -> p c k", c=HALF)
            sums = cact[:, :, SEQ:].rearrange("p c (b t) -> p c b t", b=NB)

            def spread(v):
                return v.unsqueeze(2).unsqueeze(3).to_broadcast([P, HALF, NB, NT])

            n0 = TAPS * HALF
            for k in range(TAPS + 1):
                if k < TAPS:
                    if k >= 3:
                        dve.wait_ge(conv_step, n0 + 2 * k - 3)
                    tt(ctmp[:, k % 3], hist[:, :, :, k:k + NT], spread(taps[:, :, k]), ALU.mult
                       ).then_inc(conv_step, 1)
                if k:
                    dve.wait_ge(conv_step, n0 + 2 * k - 1)
                    tt(sums, ctmp[:, (k - 1) % 3], spread(c("cb", 0, HALF)) if k == 1 else sums, ALU.add
                       ).then_inc(conv_step, 1)
            for e in range(2):
                for h in range(2):
                    emptied(dve, f"z{e}{h}")
            link(dve.memset(Z[:, :, :, 0:1], 0.0))
            flatZ = Z.rearrange("p e g c -> p (e g) c")
            per = L * 3
            with dve.Fori(0, NC // L) as i:
                for r in range(L):
                    n = 3 * r
                    src = flatZ[:, :, bass.ds(L * i + r, 1)].rearrange("p a b -> p (a b)")
                    dst = flatZ[:, :, bass.ds(L * i + r + 1, 1)].rearrange("p a b -> p (a b)")
                    tt(dve_t[:, 0, :], src, A8.rearrange("p a b -> p (a b)"), ALU.mult)
                    for e in range(2):
                        ins = tt(dve_t[:, 1, e * G:(e + 1) * G],
                                 flatZ[:, (1 - e) * G:(2 - e) * G, bass.ds(L * i + r, 1)]
                                 .rearrange("p a b -> p (a b)"), B8[:, e, :], ALU.mult)
                    ins.then_inc(scan_step, 1)
                    dve.wait_ge(scan_step, n + 1 + per * i)
                    tt(dve_t[:, 0, :], dve_t[:, 0, :], dve_t[:, 1, :], ALU.add).then_inc(scan_step, 1)
                    dve.wait_ge(scan_step, n + 2 + per * i)
                    tt(dst, dst, dve_t[:, 0, :], ALU.add).then_inc(scan_step, 1)
                    dve.wait_ge(scan_step, n + 3 + per * i)
            dve.tensor_copy(dve_t[:, 0, 0:G], Z[:, 0, :, NC]).then_inc(scan_ok, 1)
            ps = filled(dve, "ys")
            for g in range(G):
                ins = stt(Ys[:, g, :], Us[:, g, :], c("d", g), ps[:, 0, NB * g:NB * (g + 1)], ALU.mult, ALU.add)
            ins.then_inc(drained("ys"), 1)
            dve.wait_ge(h0_in, 16)
            ps = filled(dve, "zs")
            hv = h0
            link(tt(hv[:, 1], hv[:, 1], B4.unsqueeze(2).to_broadcast([P, G, NB]), ALU.mult))
            link(tt(hv[:, 0], hv[:, 0], A4.unsqueeze(2).to_broadcast([P, G, NB]), ALU.mult))
            link(tt(hv[:, 0], hv[:, 0], hv[:, 1], ALU.add))
            tt(hv[:, 0], hv[:, 0], ps[:, 0, 0:G * NB].rearrange("p (g b) -> p g b", g=G), ALU.add
               ).then_inc(drained("zs"), 1)
            ps = filled(dve, "lnm")
            for j in range(HALF):
                ins = stt(halves(cact[:, j, :]), two(ps), -1.0 / 512, halves(cact[:, j, :]), ALU.mult, ALU.add)
                if j < HALF - 1:
                    ins.then_inc(lnx_ok, 1)
            ins.then_inc(drained("lnm"), 1)
            for h in range(2):
                ps = flat(filled(dve, f"y{h}"), 1024).rearrange("p (g n) -> p g n", g=16)
                for g in range(16):
                    ins = stt(Y[:, 16 * h + g, :], U[:, 16 * h + g, :], c("d", 16 * h + g), ps[:, g, :],
                              ALU.mult, ALU.add)
                ins.then_inc(drained(f"y{h}"), 1)
            scale = float(P) ** -0.5
            for t in range(TILES):
                ps = flat(filled(dve, f"as{t}"), 1024).rearrange("p (h m) -> p h m", h=HEADS)
                link(dve.tensor_reduce(mx, ps, AX.X, ALU.max))
                ts(nmx, mx, -scale, None, ALU.mult).then_inc(max_ok, 1)
                emptied(dve, f"as{t}")
                link(dve.reciprocal(ars, asum))
                tt(Pm, Pm, ars.unsqueeze(2).to_broadcast([P, HEADS, MEM]), ALU.mult).then_inc(p_ok, 1)
                if t == 0:
                    ps = filled(dve, "lnv")
                    ts(halves(lrs), two(ps), 1.0 / 512, LN_EPS, ALU.mult, ALU.add).then_inc(drained("lnv"), 1)
                    dve.wait_ge(lr_ok, 1)
                    link(dve.reciprocal(lrs, lrs))
                    for j in range(HALF):
                        stt(cact[:, j, :], cact[:, j, :], c("lg", j), lrs, ALU.mult, ALU.mult).then_inc(lnx_ok, 1)
            ps = filled(dve, "ss_t")
            link(dve.tensor_reduce(mx[:, 0:1], ps[:, 0, 0:MEM], AX.X, ALU.max))
            ts(nmx[:, 0:1], mx[:, 0:1], -scale, None, ALU.mult).then_inc(max_ok, 1)
            emptied(dve, "ss_t")
            link(dve.reciprocal(ars[:, 0:1], asum[:, 0:1]))
            ts(Ps, Ps, ars[:, 0:1], None, ALU.mult).then_inc(p_ok, 1)
            def split(src, high, rest, before, done):
                ts(rest, src, 1.0, None, ALU.mult).then_inc(split_step, 1)
                dve.wait_ge(split_step, 2 * before + 1)
                tt(rest, src, rest.bitcast(F32), ALU.subtract).then_inc(split_step, 1)
                dve.wait_ge(split_step, 2 * before + 2)
                ts(high, src, 1.0, None, ALU.mult).then_inc(done, 1)

            def gate_weights(b, q):
                ld = WGATE0 + b
                dve.wait_ge(w_in[ld % WS], 16 * (ld // WS + 1) + 16 * q)
                dst = low(b)
                k = dst.shape[1]
                return wring[:, ld % WS, 0:k], whigh[:, ld % WS, 0:k], dst

            def out_weights(j):
                slot, n = LOAD[f"o{j}"]
                dve.wait_ge(w_in[slot], 16 * (n + 1))
                return wring[:, slot, :], whigh[:, slot, :], wl[:, 1024 * (j % 4):1024 * (j % 4) + 1024]

            n_split = 0
            dve.wait_ge(y_in, 16)
            for k in range(KD):
                split(nT[:, k, :], nTh[:, k, :], nTl[:, k, :], n_split, nl_ok)
                n_split += 1

            def split_first(b):
                split(*gate_weights(b, 0), n_split, wl_ok)
                return n_split + 1

            for b in range(2):
                n_split = split_first(b)
            def split_branch(src, high, rest, before):
                for j in range(HALF):
                    split(src[:, j, :], high[:, j, :], rest[:, j, :], before + j, bl_ok)
                return before + HALF

            dve.wait_ge(cact_ok, HALF)
            emptied(dve, "ss_o")
            dve.wait_ge(state_out, 32)
            n_split = split_branch(cact, ch, cl, n_split)
            n_split = split_branch(qT, qh, ql, n_split)
            n_split = split_first(2)
            for j in range(HALF):
                p, n = JOB[f"glu{j}"]
                dve.wait_ge(free[p], n + 1)
                tt(zg[:, j, :], zg[:, j, :], zz[:, j, :], ALU.mult).then_inc(zg_ok, 1)
            dve.wait_ge(zg_ok, HALF)
            n_split = split_branch(zg, zh, zl, n_split)
            for b in range(3, 6):
                n_split = split_first(b)
            mflat = merged.rearrange("p k t -> p (k t)")
            mlflat, mhflat = ml.rearrange("p k t -> p (k t)"), mh.rearrange("p k t -> p (k t)")

            def merge(i, r, last=False):
                q = 2 * i + r
                dst = mflat[:, bass.ds(q * TOK, TOK)]
                for b in range(3):
                    split(*(out_weights(b) if last else gate_weights(b, q + 1)), n_split + 7 * q + b, wl_ok)
                for b in range(3):
                    gj, job = GATE0 + 6 * r + b, GATE0 + 6 * r + 3 + b
                    dve.wait_ge(free[gj % 4], gj // 4 + 1 + 3 * i)
                    dve.wait_ge(full[job % 4], job // 4 + 1 + 3 * i)
                    tt(halves(gtmp if b else dst), halves(gsg[:, r, b, :]), two(pairs[job % 4]), ALU.mult
                       ).then_inc(free[job % 4], 1)
                    dve.wait_ge(free[job % 4], job // 4 + 1 + 3 * i)
                    if b:
                        tt(dst, dst, gtmp, ALU.add).then_inc(merged_ok, 1)
                        dve.wait_ge(merged_ok, 2 * r + b + 4 * i)
                    if not last:
                        split(*gate_weights(3 + b, q + 1), n_split + 7 * q + 3 + b, wl_ok)
                split(dst, mhflat[:, bass.ds(q * TOK, TOK)], mlflat[:, bass.ds(q * TOK, TOK)], n_split + 7 * q + (3 if last else 6), ml_ok)

            with dve.Fori(0, 3) as i:
                for r in range(2):
                    merge(i, r)
            merge(3, 0)
            merge(3, 1, last=True)
            n_split += 7 * 7 + 4
            split(*out_weights(3), n_split, wl_ok)
            n_split += 1
            dve.wait_ge(x2_in, 16)
            for j in range(8):
                ps = filled(dve, f"o{j}")
                tt(halves(h2T[:, j, :]), two(ps), halves(h2T[:, j, :]), ALU.add).then_inc(drained(f"o{j}"), 1)
                if j < 4:
                    split(*out_weights(j + 4), n_split, wl_ok)
                    n_split += 1
            ps = filled(dve, "ss2")
            ts(halves(h2r), two(ps), 1.0 / D, RMS_EPS, ALU.mult, ALU.add).then_inc(drained("ss2"), 1)
            dve.wait_ge(h2r_ok, 1)
            link(dve.reciprocal(h2r, h2r))
            for k in range(KD + 1):
                if k < KD:
                    steps[0] += 1
                    stt(xbT[:, k, 0:TOK], h2T[:, k, :], c("g2", k), h2r, ALU.mult, ALU.mult).then_inc(dve_step, 1)
                if k:
                    dve.wait_ge(dve_step, steps[0] - (k < KD))
                    dve.tensor_copy(xbT[:, k - 1, TOK:].rearrange("p (r t) -> p r t", r=3),
                                    xbT[:, k - 1, SEQ:TOK].unsqueeze(1).to_broadcast([P, 3, 32])).then_inc(xbT_ok, 1)
            dve.wait_ge(iota_ok, 1)
            dve.wait_ge(state_out, 32)
            link(dve.tensor_copy(iota16, iota16.bitcast(I32)))
            link(tt(fold, ident[:, 0:32], ident[:, 32:64], ALU.add))
            link(tt(fold, fold, ident[:, 64:96], ALU.add))
            link(tt(fold, fold, ident[:, 96:128], ALU.add))

            scf = sc.rearrange("p n s k -> p (n s k)")
            expf, gatf = expert.rearrange("p n k -> p (n k)"), gate.rearrange("p n k -> p (n k)")

            def route(n, par, nth, head=None, stage=True):
                local = [0]

                def step(ins):
                    local[0] += 1
                    ins.then_inc(route_step, 1)
                    dve.wait_ge(route_step, local[0])

                if head is not None:
                    for b in (2, 3):
                        p, before = head_job(head, b)
                        dve.wait_ge(free[p], before + 1)
                dve.sem_clear(route_step)
                step(dve.tensor_copy(sw.rearrange("p s k -> p (s k)"), scf[:, bass.ds(n * 2 * P, 2 * P)]))
                for s in range(2):
                    v = sw[:, s, :]
                    step(dve.max(tv[:, s, 0:8], v))
                    step(dve.max_index(tiu[:, s, 0:8], tv[:, s, 0:8], v))
                    step(dve.match_replace(v, tv[:, s, 0:8], v, NEG))
                    step(dve.max(tv[:, s, 8:16], v))
                    step(dve.max_index(tiu[:, s, 8:16], tv[:, s, 8:16], v))
                step(tt(cand, tv[:, 0, :].unsqueeze(2).to_broadcast([P, 16, 16]),
                        tv[:, 1, :].unsqueeze(1).to_broadcast([P, 16, 16]), ALU.add))
                cf = cand.rearrange("p a b -> p (a b)")
                step(dve.max(cv[:, 0:8], cf))
                step(dve.max_index(ciu[:, 0:8], cv[:, 0:8], cf))
                step(dve.match_replace(cf, cv[:, 0:8], cf, NEG))
                step(dve.max(cv[:, 8:16], cf))
                step(dve.max_index(ciu[:, 8:16], cv[:, 8:16], cf))
                step(ts(hlu[:, 0, :], ciu, 4, None, ALU.logical_shift_right))
                step(ts(hlu[:, 1, :], ciu, 15, None, ALU.bitwise_and))
                step(dve.tensor_copy(hlf, hlu))
                step(dve.tensor_copy(tif, tiu))
                step(dve.tensor_copy(i12[:, 0, 0:1], cv[:, 0:1]))
                ts(cv, cv, i12[:, 0, 0:1], None, ALU.subtract).then_inc(cdiff, 1)
                dve.wait_ge(cdiff, nth + 1)
                for s in range(2):
                    step(tt(eq, hlf[:, s, :].unsqueeze(2).to_broadcast([P, 16, 16]),
                            iota16.unsqueeze(1).to_broadcast([P, 16, 16]), ALU.is_equal))
                    step(tt(eq, eq, tif[:, s, :].unsqueeze(1).to_broadcast([P, 16, 16]), ALU.mult))
                    step(dve.tensor_reduce(i12[:, s, :], eq, AX.X, ALU.add))
                step(stt(i12[:, 0, :], i12[:, 0, :], 128.0, i12[:, 1, :], ALU.mult, ALU.add))
                step(dve.tensor_copy(expf[:, bass.ds(n * TOPK, TOPK)], i12[:, 0, :]))
                dve.wait_ge(cexp, nth + 1)
                step(dve.reciprocal(ers, esum))
                step(ts(gatf[:, bass.ds(n * TOPK, TOPK)], ce, ers, None, ALU.mult))
                if stage:
                    dve.tensor_copy(idx_u[:, par, :], i12[:, 0, :]).then_inc(routed, 1)
                    dve.wait_ge(routed, n + 1)

            def dot(n, par, x, first, last):
                for j in range(first, last):
                    dve.wait_ge(u_in[j % RING], 32 * n + 16 * (j // RING + 1))
                    u = uring[:, j % RING, :]
                    dve.tensor_tensor_reduce(u, u, x, 1.0, 0.0, ALU.mult, ALU.add, dots[:, par, j:j + 1]
                                             ).then_inc(u_used, 1)

            def weigh(n, par):
                dve.wait_ge(gel_ok, n + 1)
                w = gatf[:, bass.ds(n * TOPK, TOPK)]
                tt(w, w, gel[:, par, :], ALU.mult).then_inc(w_ok, 1)

            def stage_v(n, par):
                dve.tensor_copy(idx_v[:, par, :], expf[:, bass.ds(n * TOPK, TOPK)]).then_inc(idxv_ok, 1)

            def add_v(n, par, t):
                if not (isinstance(n, int) and n == 0):
                    dve.wait_ge(acc_step, n)
                dve.wait_ge(v_used, TOPK * n + TOPK)
                tt(h2[:, t, :], h2[:, t, :], flat(pairs[par], 1024), ALU.add).then_inc(acc_step, 1)

            def finish(t, rows):
                dve.wait_ge(acc_step, min(PH * (t + 1), PH * TILES + 1))
                dve.sem_inc(acc_ok, 1)
                dve.wait_ge(fsq_ok, t + 1)
                ts(frs[0:rows, :], fss[0:rows, :], 1.0 / D, RMS_EPS, ALU.mult, ALU.add).then_inc(fms_ok, 1)
                dve.wait_ge(frt_ok, t + 1)
                link(dve.reciprocal(frs[0:rows, :], frs[0:rows, :]))
                stt(ytile[0:rows, :], h2[0:rows, t, :], frs[0:rows, 0:1], gf[0:rows, :], ALU.mult, ALU.mult
                    ).then_inc(yt_ok, 1)

            for t in range(TILES + 1):
                emptied(dve, f"ht{t}")
            for n in range(LAG):
                route(n, n, n, n)
            for t in range(TILES + 1):
                emptied(dve, f"xt{t}")

            def step(n, r, t, t_lag, nth=None, head=None, sample=None):
                dot(n, r, xb[:, t, :], 0, TOPK // 2)
                if not (isinstance(n, int) and n <= LAG):
                    add_v(n - LAG - 1, 1 - r, t_lag)
                    stage_v(n - 1, 1 - r)
                dot(n, r, xb[:, t, :], TOPK // 2, TOPK)
                if nth is not None:
                    route(n + LAG, r, nth, head)
                weigh(n, r)
                if sample is not None:
                    route(sample, r, nth + 1, stage=False)
                if isinstance(n, int) and n < LAG:
                    stage_v(n, r)

            for n in range(PH):
                step(n, n % 2, 0, 0, n + LAG, n + LAG if n + LAG < PH else None)
            dve.wait_ge(gf_in, 16)
            for t, nth, sample in ((1, lambda n: n + LAG, lambda n: None),
                                   (2, lambda n: 2 * n + LAG - 2 * PH, lambda n: n + 2 * PH),
                                   (3, lambda n: n + LAG + PH, lambda n: None)):
                for n in range(PH * t, PH * t + 4):
                    step(n, n % 2, t, t - 1 if n <= PH * t + LAG else t, nth(n), None, sample(n))
                    if n == PH * t + LAG:
                        finish(t - 1, P)
                with dve.Fori(4 * t + 2, 4 * t + 4 - (t == 3)) as i:
                    for r in range(2):
                        n = 2 * i + r
                        step(n, r, t, t, nth(n), None, sample(n))
                if t == 2:
                    ef = expf[:, TILES * PH * TOPK:].rearrange("p (j q) -> p j q", q=4)
                    gq = gatf[:, TILES * PH * TOPK:].rearrange("p (j q) -> p j q", q=4)
                    for q in range(4):
                        rows = slice(32 * q, 32 * q + 32)
                        dve.tensor_copy(idx_s[rows, :], ef[rows, :, q])
                        ins = dve.tensor_copy(gate_s[rows, :], gq[rows, :, q])
                    ins.then_inc(samples_routed, 1)
            for r in range(2):
                step(TILES * PH - LAG + r, r, TILES - 1, TILES - 1)
            for j in range(32):
                if j == TOPK // 2:
                    add_v(TILES * PH - LAG - 1, 1, TILES - 1)
                    stage_v(TILES * PH - 1, 1)
                dve.wait_ge(u_in[j % RING], 16 * (2 * TILES * PH + j // RING + 1))
                u = uring[:, j % RING, :]
                dve.tensor_tensor_reduce(u, u, xb[:, TILES, :], 1.0, 0.0, ALU.mult, ALU.add,
                                         dots.rearrange("p a b -> p (a b)")[:, j:j + 1]).then_inc(u_used, 1)
            dve.wait_ge(gel_ok, TILES * PH + 1)
            dve.wait_ge(samples_routed, 1)
            tt(gate_s, gate_s, gel.rearrange("p a b -> p (a b)"), ALU.mult).then_inc(w_ok, 1)
            for r in range(2):
                add_v(TILES * PH - LAG + r, r, TILES - 1)
            finish(TILES - 1, P)
            dve.wait_ge(v_used, TOPK * TILES * PH + 32)
            tt(h2[0:32, TILES, :], h2[0:32, TILES, :], flat(pairs[0], 1024)[0:32, :], ALU.add).then_inc(acc_step, 1)
            dve.wait_ge(yt_ok, TILES)
            finish(TILES, NB * NT)


OUTS = (("y", (TOK, D)), ("ssm_p", (P, G)), ("ssm_s", (P, G, NB)), ("conv_p", (P, HALF, PAD)),
        ("conv_s", (P, HALF, NB, PAD)), ("mem_k", (P, HEADS, MEM)), ("mem_v", (P, 2, 512)))


def kernel(x_prompt, x_sample, mem_prompt, state_ssm_re, state_ssm_im, state_conv,
           cache_mem_k, cache_mem_v, norm1_g, w_in, b_in, s5_log_dt, s5_a_re, s5_a_im,
           s5_b_re, s5_b_im, s5_c_re, s5_c_im, s5_d, s5_glu_w, s5_glu_b, w_s5_proj,
           conv_dw_w, conv_dw_b, conv_ln_g, conv_ln_b, w_conv_proj, mem_norm_g,
           w_mem_k, w_mem_v, w_xa_proj, w_out, norm2_g, peer_w_q, peer_sub_keys,
           peer_u, peer_v, final_norm_g):
    import numpy as np
    import concourse.bacc as bacc
    from concourse.bass_utils import run_bass_kernel_spmd

    def cols(v):
        return np.asarray(v).reshape(-1, P).T

    def blocks(w):
        w = np.asarray(w)
        k, m = w.shape
        return np.ascontiguousarray(w.reshape(k // P, P, m // P, P).transpose(2, 1, 0, 3)).reshape(m // P, P, k)

    def stack(re, im):
        re, im = np.asarray(re), np.asarray(im)
        return np.concatenate([np.moveaxis(re, 1, 0), np.moveaxis(im, 1, 0)], 0)

    x = np.concatenate([np.asarray(x_prompt)[0], np.asarray(x_sample).reshape(NB * NT, D)], 0)
    conv_w = np.asarray(conv_dw_w)[0].T.reshape(HALF, P, TAPS).transpose(1, 0, 2).reshape(P, HALF * TAPS)
    keys = np.asarray(peer_sub_keys)[0].transpose(2, 0, 1).reshape(P, 2 * P)
    d_rows = np.tile(np.asarray(s5_d)[0].T, (L, 1))
    consts = np.concatenate([cols(b_in[0]), cols(norm1_g[0]), cols(mem_norm_g[0]), cols(norm2_g[0]),
                             cols(s5_glu_b[0]), conv_w, cols(conv_dw_b[0]), cols(conv_ln_g[0]),
                             cols(conv_ln_b[0]), d_rows, keys], 1)
    br, bi, cr, ci = (np.asarray(v)[0] for v in (s5_b_re, s5_b_im, s5_c_re, s5_c_im))
    cr, ci = cr.transpose(0, 2, 1), ci.transpose(0, 2, 1)
    ar, ai = np.asarray(s5_a_re)[0], np.asarray(s5_a_im)[0]
    s5 = np.concatenate([np.tile(np.asarray(s5_log_dt), (P, 1)), stack(ar, ar), stack(ai, ai)]
                        + [stack(*v).reshape(P, G * CG) for v in ((br, bi), (bi, br), (cr, ci), (ci, cr))], 1)
    hr, hi = (np.asarray(v)[0].transpose(1, 2, 0) for v in (state_ssm_re, state_ssm_im))
    given = {
        "x_t": x.T.reshape(KD, P, TOK).transpose(1, 0, 2),
        "mem_t": np.asarray(mem_prompt)[0].T.reshape(KD, P, MEM).transpose(1, 0, 2),
        "consts": consts, "s5_pack": s5,
        "h0": np.stack([stack(hr, hi), stack(hi, hr)], 1).reshape(P, 2 * G * NB),
        "conv_hist": np.asarray(state_conv)[0].transpose(2, 0, 1).reshape(HALF, P, NB, PAD).transpose(1, 0, 2, 3),
        "cache_k": np.asarray(cache_mem_k)[0].transpose(0, 3, 2, 1).reshape(NB, P, HEADS * MEM),
        "cache_v": np.asarray(cache_mem_v)[0].reshape(NB, 2, P, 512).transpose(0, 2, 1, 3).reshape(NB, P, 1024),
        "w_in": blocks(w_in[0]), "w_mem_k": blocks(w_mem_k[0]), "w_mem_v": blocks(w_mem_v[0]),
        "glu_w": blocks(s5_glu_w[0]),
        "proj": np.stack([blocks(w[0]) for w in (w_s5_proj, w_conv_proj, w_xa_proj)]),
        "w_out": blocks(w_out[0]), "peer_q": blocks(peer_w_q[0]),
        "peer_u": np.asarray(peer_u)[0], "peer_v": np.asarray(peer_v)[0],
        "final_g": np.asarray(final_norm_g),
    }
    nc = bacc.Bacc("TRN2", target_bir_lowering=False, num_devices=1)
    given = {f"in_{k}": np.ascontiguousarray(v) for k, v in given.items()}
    a = {k[3:]: nc.dram_tensor(k, v.shape, mybir.dt.from_np(v.dtype), kind="ExternalInput").ap()
         for k, v in given.items()}
    o = {k: nc.dram_tensor(f"out_{k}", shape, F32, kind="ExternalOutput").ap() for k, shape in OUTS}
    hybrid_step(nc, a, o)
    got = run_bass_kernel_spmd(nc, [given], core_ids=[0]).results[0]
    y, sp, ss, cp, cs, mk, mv = (np.asarray(got[f"out_{k}"]) for k, _ in OUTS)

    def rows(v):
        return v[0:N], v[N:P]

    pr, pi = (v.T.reshape(1, 1, G, N) for v in rows(sp))
    sr, si = (v.transpose(2, 1, 0).reshape(1, NB, G, N) for v in rows(ss))
    return (y[0:SEQ].reshape(1, SEQ, D), y[SEQ:].reshape(NB, NT, D), pr, pi,
            cp.transpose(2, 1, 0).reshape(1, 1, PAD, 512),
            mk.transpose(2, 1, 0).reshape(1, 1, MEM, HEADS, P),
            mv.transpose(1, 0, 2).reshape(1, 1, MEM, HEADS, P),
            sr, si, cs.transpose(2, 3, 1, 0).reshape(1, NB, PAD, 512))
```
